# Optimizing a Trainium2 kernel written in Bass

```python
import jax, jax.numpy as jnp
from jax import lax
import numpy as np

D_MODEL = 1024
BATCH = 1
SEQ = 1024
DEPTH = 1

ATTN_Q_HEADS = 8
ATTN_KV_HEADS = 2
ATTN_HEAD_DIM = 64
ATTN_GROUP = ATTN_Q_HEADS // ATTN_KV_HEADS
ATTN_WIDTH = ATTN_Q_HEADS * ATTN_HEAD_DIM
ATTN_KV_WIDTH = ATTN_KV_HEADS * ATTN_HEAD_DIM
WINDOW = 128
HGRN_HEADS = 4
HGRN_KEY_DIM = 128
HGRN_VAL_DIM = 128
HGRN_KEY_WIDTH = HGRN_HEADS * HGRN_KEY_DIM
HGRN_WIDTH = HGRN_HEADS * HGRN_VAL_DIM
HGRN_CHUNK = 64
MIX_WIDTH = ATTN_WIDTH + HGRN_WIDTH
IN_WIDTH = ATTN_WIDTH + 2 * ATTN_KV_WIDTH + 2 * HGRN_KEY_WIDTH + 2 * HGRN_WIDTH
N_EXPERTS = 32
TOP_K = 4
EXPERT_FF = D_MODEL
SWIGLU_LIMIT = 7.0
SWIGLU_ALPHA = 1.702
EXPERT_BLOCK = 128
NORM_EPS = 1e-5

kernel_name = "hymba_swa_sink_hgrn2_moe_block"

def rmsnorm(x, g):
    x32 = x.astype(jnp.float32)
    y = x32 * lax.rsqrt(jnp.mean(x32 * x32, axis=-1, keepdims=True) + NORM_EPS)
    return (y * g.astype(jnp.float32)).astype(x.dtype)

def alibi_slopes(n):
    return (2.0 ** (-8.0 * np.arange(1, n + 1) / n)).astype(np.float32)

def sliding_window_attention(q, k, v, sinks):
    B, S = q.shape[:2]
    nb = S // WINDOW
    dt = q.dtype
    qb = q.reshape(B, nb, WINDOW, ATTN_KV_HEADS, ATTN_GROUP, ATTN_HEAD_DIM)

    def band(t):
        cur = t.reshape(B, nb, WINDOW, ATTN_KV_HEADS, ATTN_HEAD_DIM)
        prev = jnp.concatenate([jnp.zeros_like(cur[:, :1]), cur[:, :-1]], axis=1)
        return jnp.concatenate([prev, cur], axis=2)

    kb, vb = band(k), band(v)
    scores = jnp.einsum('bnqhgd,bnkhd->bhgnqk', qb, kb,
                        preferred_element_type=jnp.float32) * (ATTN_HEAD_DIM ** -0.5)
    qi = jnp.arange(WINDOW)[:, None]
    ki = jnp.arange(2 * WINDOW)[None, :]
    dist = WINDOW + qi - ki
    blk = jnp.arange(nb)[:, None, None]
    valid = (dist >= 0) & (dist < WINDOW) & (blk * WINDOW - WINDOW + ki >= 0)
    slopes = jnp.asarray(alibi_slopes(ATTN_Q_HEADS)).reshape(ATTN_KV_HEADS, ATTN_GROUP)
    scores = scores - slopes[:, :, None, None, None] * dist.astype(jnp.float32)
    scores = jnp.where(valid, scores, -jnp.inf)
    sink = sinks.astype(jnp.float32).reshape(ATTN_KV_HEADS, ATTN_GROUP)[:, :, None, None, None]
    m = jnp.maximum(scores.max(axis=-1, keepdims=True), sink)
    p = jnp.exp(scores - m)
    probs = p / (p.sum(axis=-1, keepdims=True) + jnp.exp(sink - m))
    out = jnp.einsum('bhgnqk,bnkhd->bnqhgd', probs.astype(dt), vb)
    return out.reshape(B, S, ATTN_WIDTH)

def hgrn2_recurrence(q, f_logit, i, lb):
    B, S = q.shape[:2]
    f32 = jnp.float32
    nc = S // HGRN_CHUNK
    q = jax.nn.silu(q.astype(f32))
    lb = lb.astype(f32)
    f = lb + (1.0 - lb) * jax.nn.sigmoid(f_logit.astype(f32))
    logf = jnp.log(f)
    k = 1.0 - f

    def chunks(t, d):
        return t.reshape(B, nc, HGRN_CHUNK, HGRN_HEADS, d).transpose(1, 0, 3, 2, 4)

    qc = chunks(q, HGRN_KEY_DIM)
    kc = chunks(k, HGRN_KEY_DIM)
    vc = chunks(i.astype(f32), HGRN_VAL_DIM)
    bc = jnp.cumsum(chunks(logf, HGRN_KEY_DIM), axis=3)
    causal = jnp.tril(jnp.ones((HGRN_CHUNK, HGRN_CHUNK), bool))

    def step(state, inp):
        q_, k_, v_, b_ = inp
        inter = jnp.einsum('bhtk,bhkv->bhtv', q_ * jnp.exp(b_), state)
        rel = jnp.where(causal[:, :, None], b_[:, :, :, None, :] - b_[:, :, None, :, :], -jnp.inf)
        att = jnp.einsum('bhtk,bhtsk,bhsk->bhts', q_, jnp.exp(rel), k_)
        intra = jnp.einsum('bhts,bhsv->bhtv', att, v_)
        b_last = b_[:, :, -1:, :]
        new_state = (jnp.exp(b_last[:, :, 0, :, None]) * state
                     + jnp.einsum('bhsk,bhsv->bhkv', k_ * jnp.exp(b_last - b_), v_))
        return new_state, inter + intra

    s0 = jnp.zeros((B, HGRN_HEADS, HGRN_KEY_DIM, HGRN_VAL_DIM), f32)
    _, o = lax.scan(step, s0, (qc, kc, vc, bc))
    return o.transpose(1, 0, 3, 2, 4).reshape(B, S, HGRN_HEADS, HGRN_VAL_DIM)

def moe_ffn(h, router_w, router_b, w1, b1, w2, b2):
    T, D = h.shape
    f32 = jnp.float32
    logits = jnp.dot(h.astype(f32), router_w.astype(f32)) + router_b.astype(f32)
    top_v, top_e = lax.top_k(logits, TOP_K)
    gates = jax.nn.softmax(top_v, axis=-1)
    TK = T * TOP_K
    flat_e = top_e.reshape(TK)
    flat_tok = jnp.arange(TK, dtype=jnp.int32) // TOP_K
    flat_g = gates.reshape(TK)
    order = jnp.argsort(flat_e)
    se = flat_e[order]
    counts = jnp.bincount(flat_e, length=N_EXPERTS)
    padded = (counts + EXPERT_BLOCK - 1) // EXPERT_BLOCK * EXPERT_BLOCK
    start = jnp.cumsum(counts) - counts
    ends = jnp.cumsum(padded)
    pstart = ends - padded
    dest = pstart[se] + jnp.arange(TK, dtype=jnp.int32) - start[se]
    n_rows = -(-TK // EXPERT_BLOCK) * EXPERT_BLOCK + N_EXPERTS * EXPERT_BLOCK
    n_blocks = n_rows // EXPERT_BLOCK
    row_tok = jnp.zeros((n_rows,), jnp.int32).at[dest].set(flat_tok[order])
    row_gate = jnp.zeros((n_rows,), f32).at[dest].set(flat_g[order])
    block_e = jnp.clip(jnp.searchsorted(ends, jnp.arange(n_blocks) * EXPERT_BLOCK, side='right'),
                       0, N_EXPERTS - 1)
    xb = h[row_tok].reshape(n_blocks, EXPERT_BLOCK, D)

    def expert_block(args):
        xblk, e = args
        hid = jnp.dot(xblk, w1[e]) + b1[e]
        glu = jnp.minimum(hid[:, 0::2], SWIGLU_LIMIT)
        lin = jnp.clip(hid[:, 1::2], -SWIGLU_LIMIT, SWIGLU_LIMIT)
        act = glu * jax.nn.sigmoid(SWIGLU_ALPHA * glu) * (lin + 1.0)
        return jnp.dot(act, w2[e]) + b2[e]

    yb = lax.map(expert_block, (xb, block_e))
    y = jnp.zeros((T, D), f32).at[row_tok].add(
        yb.reshape(n_rows, D).astype(f32) * row_gate[:, None])
    return y.astype(h.dtype)

def setup_inputs(seed: int = 0) -> dict:
    key = jax.random.key(seed)
    ks = jax.random.split(key, 18)

    def nrm(k, shape, scale):
        return jax.random.normal(k, shape, jnp.float32) * scale

    return {
        "x": nrm(ks[0], (BATCH, SEQ, D_MODEL), 1.0),
        "norm1_g": 1.0 + nrm(ks[1], (DEPTH, D_MODEL), 0.02),
        "w_in": nrm(ks[2], (DEPTH, D_MODEL, IN_WIDTH), D_MODEL ** -0.5),
        "b_in": nrm(ks[3], (DEPTH, IN_WIDTH), 0.02),
        "attn_sinks": nrm(ks[4], (DEPTH, ATTN_Q_HEADS), 0.5),
        "attn_out_g": 1.0 + nrm(ks[5], (DEPTH, ATTN_WIDTH), 0.02),
        "hgrn_lb_logits": nrm(ks[6], (DEPTH + 1, HGRN_KEY_WIDTH), 1.0),
        "hgrn_out_g": 1.0 + nrm(ks[7], (DEPTH, HGRN_WIDTH), 0.02),
        "w_out": nrm(ks[8], (DEPTH, MIX_WIDTH, D_MODEL), MIX_WIDTH ** -0.5),
        "b_out": nrm(ks[9], (DEPTH, D_MODEL), 0.02),
        "norm2_g": 1.0 + nrm(ks[10], (DEPTH, D_MODEL), 0.02),
        "router_w": nrm(ks[11], (DEPTH, D_MODEL, N_EXPERTS), D_MODEL ** -0.5),
        "router_b": nrm(ks[12], (DEPTH, N_EXPERTS), 0.01),
        "w1": nrm(ks[13], (DEPTH, N_EXPERTS, D_MODEL, 2 * EXPERT_FF), D_MODEL ** -0.5),
        "b1": nrm(ks[14], (DEPTH, N_EXPERTS, 2 * EXPERT_FF), 0.02),
        "w2": nrm(ks[15], (DEPTH, N_EXPERTS, EXPERT_FF, D_MODEL), EXPERT_FF ** -0.5),
        "b2": nrm(ks[16], (DEPTH, N_EXPERTS, D_MODEL), 0.02),
        "final_g": 1.0 + nrm(ks[17], (D_MODEL,), 0.02),
    }

def reference(x, norm1_g, w_in, b_in, attn_sinks, attn_out_g, hgrn_lb_logits, hgrn_out_g,
              w_out, b_out, norm2_g, router_w, router_b, w1, b1, w2, b2, final_g):
    B, S, D = x.shape
    lower_bounds = jnp.cumsum(jax.nn.softmax(hgrn_lb_logits.astype(jnp.float32), axis=0), axis=0)
    split_at = list(np.cumsum([ATTN_WIDTH, ATTN_KV_WIDTH, ATTN_KV_WIDTH,
                               HGRN_KEY_WIDTH, HGRN_KEY_WIDTH, HGRN_WIDTH]))
    for l in range(DEPTH):
        h = rmsnorm(x, norm1_g[l])
        proj = jnp.dot(h, w_in[l]) + b_in[l]
        aq, ak, av, hq, hf, hi, hg = jnp.split(proj, split_at, axis=-1)
        attn = sliding_window_attention(aq, ak, av, attn_sinks[l])
        attn = rmsnorm(attn, attn_out_g[l])
        o = hgrn2_recurrence(hq, hf, hi, lower_bounds[l])
        o = o * lax.rsqrt(jnp.mean(o * o, axis=-1, keepdims=True) + NORM_EPS)
        o = o * hgrn_out_g[l].astype(jnp.float32).reshape(HGRN_HEADS, HGRN_VAL_DIM)
        o = o.reshape(B, S, HGRN_WIDTH) * jax.nn.silu(hg.astype(jnp.float32))
        mixed = jnp.concatenate([attn, o.astype(x.dtype)], axis=-1)
        x = x + jnp.dot(mixed, w_out[l]) + b_out[l]
        h2 = rmsnorm(x, norm2_g[l]).reshape(B * S, D)
        x = x + moe_ffn(h2, router_w[l], router_b[l], w1[l], b1[l], w2[l], b2[l]).reshape(B, S, D)
    return rmsnorm(x, final_g)


_drawn_inputs = setup_inputs


def setup_inputs(seed=0):
    import zlib

    import numpy as np

    out = dict(_drawn_inputs(seed))
    spreads = {}
    factors = {'hgrn_out_g': 10.508,
     'b1': 6.336,
     'b2': 7.235,
     'final_g': 23.695,
     'attn_out_g': 2.933,
     'b_out': 2.732,
     'router_b': 7.279,
     'norm2_g': 2.856}
    for name, (base, spread) in spreads.items():
        noise = np.random.default_rng([zlib.crc32(name.encode()), seed]).standard_normal(out[name].shape)
        drawn = base * np.exp(spread * noise) if base else spread * noise
        out[name] = __import__('jax').numpy.asarray(drawn.astype(out[name].dtype))
    for name, factor in factors.items():
        out[name] = (out[name] * factor).astype(out[name].dtype)
    return out
```

```python
from contextlib import ExitStack

import concourse.bass as bass
from concourse import mybir

P = 128
D = 1024
T = 1024
NT = T // P
KT = D // P
QUARTERS = 4
UNIT = 512
NQ, NKV, HD = 8, 2, 64
GROUP = NQ // NKV
HH = 4
ATTN_W = NQ * HD
C_AQ = 0
C_AK = ATTN_W
C_AV = C_AK + NKV * HD
C_HQ = C_AV + NKV * HD
C_HF = C_HQ + HH * P
C_HI = C_HF + HH * P
C_HG = C_HI + HH * P
NE = 32
TOPK = 4
FF = 1024
JOB_T = 256
JOBS = T * TOPK // JOB_T + NE - 1
JT_W = JOBS + 1
PAD_ROWS = JOB_T
EPS = 1e-5
NEG = -1e30
LIMIT = 7.0
ALPHA = 1.702
DENSE_UNITS = 8
JOB_UNITS = 6
LEVELS = 7
STEPS = LEVELS + 2
BW = 2 * FF + D
B_AV, B_HI, B_HG, B_OUT = 0, 128, 640, 1152

F32 = mybir.dt.float32
F32R = mybir.dt.float32r
I32 = mybir.dt.int32
U32 = mybir.dt.uint32
ALU = mybir.AluOpType
ACT = mybir.ActivationFunctionType
AX = mybir.AxisListType.X
SLOPES = [2.0 ** (-8.0 * (h + 1) / NQ) for h in range(NQ)]


def build(nc, x, norm1_g, w_in, b_in, attn_sinks, attn_out_g, hgrn_lb_logits, hgrn_out_g, w_out,
          b_out, norm2_g, router_w, router_b, w1, b1, w2, b2, final_g, out):
    x, out = x[0], out[0]
    w_in, w_out, w1, w2 = w_in[0], w_out[0], w1[0], w2[0]
    KB = 1024
    base = (nc.sbuf_base + 31) // 32 * 32

    def at(name, offset, shape, dt=F32):
        return nc.alloc_sbuf_tensor_at(name, shape, dt, offset=base + int(offset))

    def dram(name, shape, dt=F32):
        return nc.dram_tensor(name, shape, dt, kind="Internal").ap()

    h2_d = dram("h2_d", (T + PAD_ROWS, D))
    acc_d = dram("acc_d", (T + PAD_ROWS, D))
    table_d = dram("table_d", (NE * T, 2))
    hg_d = dram("hg_d", (T, 512))
    brow_d = dram("brow_d", (NE + 1, 2, BW))

    raw = at("raw", 0, [P, QUARTERS, 2, UNIT])
    whi = at("whi", 16 * KB, [P, QUARTERS, 2, UNIT], F32R)
    wlo = at("wlo", 32 * KB, [P, QUARTERS, 2, UNIT], F32R)
    A = 48 * KB
    th = at("th", A, [P, KT, T], F32R)
    tl = at("tl", A + 32 * KB, [P, KT, T], F32R)
    mix = at("mix", A, [P, NT, D])
    alibi = at("alibi", A + 32 * KB, [P, NQ, 2 * P])
    score = at("score", A + 40 * KB, [P, 2, GROUP, 2 * P])
    probT = at("probT", A + 48 * KB, [P, 2, GROUP, P])
    hk = at("hk", A + 32 * KB, [P, HH, T])
    reset = at("reset", A + 52 * KB, [P, T])
    attT = [at("attT0", A + 48 * KB, [P, NT, P]), at("attT1", A + 56 * KB, [P, NT, P])]
    stat = at("stat", A + 60 * KB, [P, 6, 2 * NT, GROUP])
    hgt = at("hgt", A + 32 * KB, [P, NT, 512])
    junk = at("junk", A + 48 * KB, [P, D])
    h2 = at("h2", A + 32 * KB, [P, 2, D])
    h2Th = at("h2Th", A + 40 * KB, [P, KT, P], F32R)
    h2Tl = at("h2Tl", A + 44 * KB, [P, KT, P], F32R)
    g2row = at("g2row", A + 52 * KB, [P, D])
    zero = at("zero", A + 56 * KB, [P, D])
    B = 112 * KB
    xs = at("xs", B, [P, NT, D])
    bp = at("bp", B + 32 * KB, [NE + 1, BW])
    bph = at("bph", B + 44 * KB, [NE + 1, BW], F32R)
    bpl = at("bpl", B + 56 * KB, [NE + 1, BW], F32R)
    tinit = at("tinit", B + 68 * KB, [P, JOB_T, 2])
    hf = at("hf", B, [P, HH, T])
    hq = at("hq", B + 16 * KB, [P, HH, T])
    hv = at("hv", B + 32 * KB, [P, NT, 512])
    aq = at("aq", B + 48 * KB, [P, GROUP, T])
    ak = at("ak", B + 64 * KB, [P, P + T])
    av = at("av", B + 68.5 * KB, [P, NT, P])
    he = at("he", B + 48 * KB, [P, 2, T])
    hp = at("hp", B + 56 * KB, [P, 2, T])
    kbT = at("kbT", B + 64 * KB, [P, NT, P])
    state = at("state", B + 68 * KB, [P, NT, P])
    mh = at("mh", B, [P, KT, T], F32R)
    ml = at("ml", B + 32 * KB, [P, KT, T], F32R)
    xTh = at("xTh", B, [P, KT, 2, P], F32R)
    xTl = at("xTl", B + 8 * KB, [P, KT, 2, P], F32R)
    aTh = at("aTh", B + 16 * KB, [P, KT, 2, P], F32R)
    aTl = at("aTl", B + 24 * KB, [P, KT, 2, P], F32R)
    xg = at("xg", B + 32 * KB, [P, 2, D])
    y = at("y", B + 40 * KB, [P, 2, D])
    glu = at("glu", B + 48 * KB, [P, 2, 256])
    lin = at("lin", B + 50 * KB, [P, 2, 256])
    sig = at("sig", B + 52 * KB, [P, 2, 256])
    R = [B + 72.5 * KB]

    def rest(name, shape, dt=F32):
        words = 1
        for n in shape[1:]:
            words *= n
        tensor = at(name, R[0], shape, dt)
        R[0] += (words * 4 + 31) // 32 * 32
        return tensor

    junk0 = at("junk0", R[0], [P, D])
    brow = rest("brow", [2, BW], F32R)
    grow = rest("grow", [P, D])
    hgs = at("hgs", R[0] - 4 * KB, [P, 2, 512])
    ident = rest("ident", [P, P])
    epsc = rest("epsc", [P, 1])
    ones2 = rest("ones2", [2, P], F32R)
    dist = rest("dist", [P, 2 * P])
    closed = rest("closed", [P, 2 * P])
    maskL = rest("maskL", [P, LEVELS, 64], I32)
    before = at("before", R[0], [P, P])
    onesf = at("onesf", R[0] + 512, [P, P])
    R[0] += 1024
    bcol = rest("bcol", [P, 13])
    sinks = rest("sinks", [P, NQ])
    lbl = rest("lbl", [P, 2, HH])
    lbe = rest("lbe", [P, 2, HH])
    lbm = rest("lbm", [P, HH])
    lb = rest("lb", [P, HH])
    oml = rest("oml", [P, HH])
    ss = rest("ss", [P, NT])
    rstd = rest("rstd", [P, NT])
    decay = rest("decay", [P, NT])
    ssa = rest("ssa", [P, NT, 5])
    rsa = rest("rsa", [P, NT, 5])
    assert base + R[0] <= nc.sbuf_usable_end, R[0] / KB
    Z = [A + 60 * KB]

    def late(name, shape, dt=F32):
        words = 1
        for n in shape[1:]:
            words *= n
        tensor = at(name, Z[0], shape, dt)
        Z[0] += (words * 4 + 31) // 32 * 32
        assert Z[0] <= A + 64 * KB
        return tensor

    rb = late("rb", [P, NE])
    iotaE = late("iotaE", [P, NE])
    logit = late("logit", [P, NE])
    top = late("top", [P, 8])
    topi = late("topi", [P, 8], U32)
    topf = late("topf", [P, 8])
    ntop = late("ntop", [P, 1])
    gexp = late("gexp", [P, TOPK])
    gden = late("gden", [P, 1])
    grec = late("grec", [P, 1])
    hot = late("hot", [P, TOPK, NE])
    count = late("count", [P, NT + 1, NE])
    picked = late("picked", [P, NE])
    rank = late("rank", [P, TOPK])
    posf = late("posf", [P, TOPK])
    tok = late("tok", [P, NT])
    B2 = B + 66 * KB
    rw = at("rw", B2, [P, KT, NE])
    rwh = at("rwh", B2 + KB, [P, KT, NE], F32R)
    rwl = at("rwl", B2 + 2 * KB, [P, KT, NE], F32R)
    pos = at("pos", B2 + 3 * KB, [P, NT, TOPK], I32)
    load = at("load", B2 + 3.25 * KB, [P, NT, TOPK, 2])
    nexp = at("nexp", B2 + 3.5 * KB, [NE, 4])
    eid = at("eid", B2 + 3.53125 * KB, [NE, 1])
    jobi = at("jobi", B2 + 3.5625 * KB, [NE, JT_W])
    jobm = at("jobm", B2 + 3.75 * KB, [NE, 2, JT_W])
    jobr = at("jobr", B2 + 4.25 * KB, [NE, 3, JT_W])
    jobt = at("jobt", B2 + 5 * KB, [1, 3, JT_W], I32)
    tnext = at("tnext", B2 + 5.75 * KB, [P, 2, 2])
    inext = at("inext", B2 + 5.78125 * KB, [P, 2], I32)
    icur = at("icur", B2 + 5.8125 * KB, [P, 2], I32)
    gcur = at("gcur", B2 + 5.84375 * KB, [P, 2])

    ctx = ExitStack()
    with ctx:
        ps = ctx.enter_context(nc.psum_tensor("ps", [P, 8, 512], F32))

        def sem(name):
            return ctx.enter_context(nc.semaphore(name))

        x_in = [sem(f"x_in{t}") for t in range(NT)]
        const_in, bias_in, bias_hi, bias_lo, bias_out, brow_in = (
            sem(n) for n in ("const_in", "bias_in", "bias_hi", "bias_lo", "bias_out", "brow_in"))
        bp_zero, tinit_done, tinit_out, const_set, pool_step, dve_step, act_step = (
            sem(n) for n in ("bp_zero", "tinit_done", "tinit_out", "const_set", "pool_step",
                             "dve_step", "act_step"))
        lb_max, lb_exp, lb_set = sem("lb_max"), sem("lb_exp"), sem("lb_set")
        squared, normed, turned, turned_hi, turned_lo = (
            sem(n) for n in ("squared", "normed", "turned", "turned_hi", "turned_lo"))
        raw_in = [sem(f"raw_in{q}") for q in range(QUARTERS)]
        split_hi, split_lo_dve, split_lo_pool, quarter_used = (
            sem(n) for n in ("split_hi", "split_lo_dve", "split_lo_pool", "quarter_used"))
        chain_done, taken_act, taken_dve = sem("chain_done"), sem("taken_act"), sem("taken_dve")
        act_part = sem("act_part")
        hg_ready = sem("hg_ready")
        hg_out = [sem("hg_out0"), sem("hg_out1")]
        ak_zero, alibi_set = sem("ak_zero"), sem("alibi_set")
        scored, score_added, maxed, exped, sinked, probs_turned, pT_act, pT_dve, heads_done, heads_out = (
            sem(n) for n in ("scored", "score_added", "maxed", "exped", "sinked", "probs_turned",
                             "pT_act", "pT_dve", "heads_done", "heads_out"))
        reset_set, keys_set, logs_set, sums_set = (
            sem(n) for n in ("reset_set", "keys_set", "logs_set", "sums_set"))
        arg_set, exp_set, prod_dve, prod_pool, diag_done, level_used, level_copied = (
            sem(n) for n in ("arg_set", "exp_set", "prod_dve", "prod_pool", "diag_done",
                             "level_used", "level_copied"))
        kbT_set, added_state, states_set, rec_out = (
            sem(n) for n in ("kbT_set", "added_state", "states_set", "rec_out"))
        gmix_in, hgt_in, hgt_set, msq, mnormed, mturned, mturned_hi, mturned_lo = (
            sem(n) for n in ("gmix_in", "hgt_in", "hgt_set", "msq", "mnormed", "mturned",
                             "mturned_hi", "mturned_lo"))
        xr_in, late_in, late_set, x2_set, sq2, h2_set, h2_turned, h2_hi, h2_lo = (
            sem(n) for n in ("xr_in", "late_in", "late_set", "x2_set", "sq2", "h2_set",
                             "h2_turned", "h2_hi", "h2_lo"))
        h2_out = [sem("h2_out0"), sem("h2_out1")]
        acc_out, pads_out, zero_set, logits_done, top_set, gate_exp, picked_set, ranked, pos_set = (
            sem(n) for n in ("acc_out", "pads_out", "zero_set", "logits_done", "top_set",
                             "gate_exp", "picked_set", "ranked", "pos_set"))
        rw_hi, rw_lo, table_out = sem("rw_hi"), sem("rw_lo"), sem("table_out")
        jn, jn_set, jbase, jrows, jsum, jobs_set = (
            sem(n) for n in ("jn", "jn_set", "jbase", "jrows", "jsum", "jobs_set"))
        tnext_in, tnext_cast, gathered, tcur_set = (
            sem(n) for n in ("tnext_in", "tnext_cast", "gathered", "tcur_set"))
        brow1_in, brow2_in = sem("brow1_in"), sem("brow2_in")
        hid_taken, glu_set, sig_set, act_set, jobs_over = (
            sem(n) for n in ("hid_taken", "glu_set", "sig_set", "act_set", "jobs_over"))
        aT_hi, aT_lo, x_turned, xT_hi, xT_lo, y_set, scattered = (
            sem(n) for n in ("aT_hi", "aT_lo", "x_turned", "xT_hi", "xT_lo", "y_set",
                             "scattered"))
        a_turned = [sem("a_turned0"), sem("a_turned1")]
        swish_set, rooted, eps_set = sem("swish_set"), sem("rooted"), sem("eps_set")
        pool_mark, sync_mark = sem("pool_mark"), sem("sync_mark")
        fin_in = [sem(f"fin_in{t}") for t in range(NT)]
        gfin_in, fsq, fset, fin_out = sem("gfin_in"), sem("fsq"), sem("fset"), sem("fin_out")

        CHAINS = [8, 8, 8, 4, 8, 8, 8, 8]
        BEFORE = [sum(CHAINS[:n]) for n in range(DENSE_UNITS + 1)]

        BY_ACT = [8, 8, 0, 2, 8, 8, 0, 0]
        BY_DVE = [0, 8, 8, 2, 0, 8, 8, 8]

        def taken(n, c):
            if n in (0, 4) or (n == 3 and c >= 2):
                return taken_act, sum(BY_ACT[:n]) + c + 1 - (2 if n == 3 else 0)
            return taken_dve, sum(BY_DVE[:n]) + c + 1

        def args_by(s):
            return (LEVELS + 1) * (s // STEPS) + min(s % STEPS, LEVELS) + 1

        def dve_prods_by(s):
            return (LEVELS + 1) * (s // STEPS) + (s % STEPS) + (s % STEPS < LEVELS)

        def pool_prods_by(s):
            return (LEVELS + 1) * (s // STEPS) + min(s % STEPS, LEVELS) + 1

        def chain_ready(engine, n, c):
            if c < CHAINS[n] - 1:
                engine.wait_ge(chain_done, BEFORE[n] - n + c + 1)
            else:
                engine.wait_ge(quarter_used, 4 * n + 4)

        N_CONST = 2 + 5 + 1 + 1
        U_COLS = [C_HF, C_HQ, C_AQ, C_AK, C_HI, C_HG, 0, UNIT]
        wiv = w_in.rearrange("(q a p) n -> q p a n", q=QUARTERS, p=P)
        wov = w_out.rearrange("(q a p) n -> q p a n", q=QUARTERS, p=P)
        w1v = w1.rearrange("e (q a p) n -> q e p a n", q=QUARTERS, p=P)
        w2v = w2.rearrange("e (q a p) n -> q e p a n", q=QUARTERS, p=P)
        
        def expert_part(view, q, e, cols):
            return view[q, bass.ds(e, 1), :, :, cols].rearrange("o p a n -> (o p) a n")

        def bias_part(e, cols):
            return brow_d[bass.ds(e, 1), :, cols].rearrange("o s n -> (o s) n")

        bview = b_in[0]

        block = ctx.enter_context(nc.Block())

        @block.sync
        def _(sp):
            sp.dma_start(xs[:, 0, :], x[0:P, :]).then_inc(x_in[0], 16)
            sp.dma_start(grow[:, :], norm1_g.broadcast_to([P, D])).then_inc(const_in, 16)
            sp.dma_start(sinks[:, :], attn_sinks.broadcast_to([P, NQ])).then_inc(const_in, 16)
            for t in range(1, 3):
                sp.dma_start(xs[:, t, :], x[t * P:(t + 1) * P, :]).then_inc(x_in[t], 16)

            def weights(n, q):
                cols = 256 if n == 3 else UNIT
                src = wiv if n < 6 else wov
                if n == 2:
                    for a in range(2):
                        for g in range(NKV):
                            sp.dma_start(raw[:, q, a, :].rearrange("p (i g d) -> p g i d", g=NKV, i=GROUP)[:, g],
                                         wiv[q, :, a, 256 * g:256 * g + 256].rearrange("p (i d) -> p i d", i=GROUP)
                                         ).then_inc(raw_in[q], 16)
                    return
                sp.dma_start(raw[:, q, :, 0:cols],
                             src[q, :, :, U_COLS[n]:U_COLS[n] + cols]).then_inc(raw_in[q], 16)

            def raw_free(g, q):
                sp.wait_ge(split_hi, 4 * g + q - 3)
                if q < 3:
                    sp.wait_ge(split_lo_dve, 3 * g + q - 2)
                else:
                    sp.wait_ge(split_lo_pool, g)

            for g in range(NKV):
                sp.dma_start(bcol[64 * g:64 * g + 64, 0:4],
                             bview[g * 256:g * 256 + 256].rearrange("(i p) -> p i", p=64),
                             allow_slow_non_contiguous=True).then_inc(const_in, 16)
            sp.dma_start(bcol[:, 4:5], bview[C_AK:C_AK + P].rearrange("(i p) -> p i", p=P),
                         allow_slow_non_contiguous=True).then_inc(const_in, 16)
            sp.dma_start(bcol[:, 5:9], bview[C_HQ:C_HQ + 512].rearrange("(i p) -> p i", p=P),
                         allow_slow_non_contiguous=True).then_inc(const_in, 16)
            sp.dma_start(bcol[:, 9:13], bview[C_HF:C_HF + 512].rearrange("(i p) -> p i", p=P),
                         allow_slow_non_contiguous=True).then_inc(const_in, 16)
            sp.dma_start(lbl[:, 0, :], hgrn_lb_logits[0].rearrange("(h p) -> p h", p=P),
                         allow_slow_non_contiguous=True).then_inc(const_in, 16)
            sp.dma_start(lbl[:, 1, :], hgrn_lb_logits[1].rearrange("(h p) -> p h", p=P),
                         allow_slow_non_contiguous=True).then_inc(const_in, 16)
            for q in range(QUARTERS):
                weights(0, q)
            for t in range(3, NT):
                sp.dma_start(xs[:, t, :], x[t * P:(t + 1) * P, :]).then_inc(x_in[t], 16)
            sp.wait_ge(bp_zero, 1)
            sp.dma_start(bp[0:NE, 0:2 * FF], b1[0]).then_inc(bias_in, 16)
            sp.dma_start(bp[0:NE, 2 * FF:BW], b2[0]).then_inc(bias_in, 16)
            sp.dma_start(bp[NE:NE + 1, 0:128], b_in[:, C_AV:C_HQ]).then_inc(bias_in, 16)
            sp.dma_start(bp[NE:NE + 1, 128:1152], b_in[:, C_HI:C_HI + D]).then_inc(bias_in, 16)
            sp.dma_start(bp[NE:NE + 1, 1152:2176], b_out).then_inc(bias_in, 16)
            for q in range(QUARTERS):
                raw_free(1, q)
                weights(1, q)
            sp.wait_ge(bias_hi, 1)
            sp.dma_start(brow_d[:, 0, :], bph[:, :].bitcast(F32)).then_inc(bias_out, 16)
            sp.wait_ge(bias_lo, 1)
            sp.dma_start(brow_d[:, 1, :], bpl[:, :].bitcast(F32)).then_inc(bias_out, 16)
            sp.wait_ge(bias_out, 32)
            sp.dma_start(brow[:, :].bitcast(F32), brow_d[NE]).then_inc(brow_in, 16)
            for n in range(2, 7):
                for q in range(QUARTERS):
                    raw_free(n, q)
                    weights(n, q)
            sp.wait_ge(hg_out[0], 16 * 4)
            sp.wait_ge(hg_out[1], 16 * 4)
            sp.dma_start(grow[:, 0:512], attn_out_g.broadcast_to([P, 512])).then_inc(gmix_in, 16)
            sp.dma_start(grow[:, 512:D], hgrn_out_g.broadcast_to([P, 512])).then_inc(gmix_in, 16)
            sp.wait_ge(level_used, STEPS * HH)
            sp.wait_ge(prod_pool, pool_prods_by(STEPS * HH - 1))
            sp.wait_ge(rec_out, 2 * HH)
            sp.dma_start(hgt[:, :, :], hg_d.rearrange("(t p) n -> p t n", p=P)).then_inc(hgt_in, 16)
            sp.dma_start(g2row[:, :], norm2_g.broadcast_to([P, D])).then_inc(late_in, 16)
            sp.dma_start(rb[:, :], router_b.broadcast_to([P, NE])).then_inc(late_in, 16)
            sp.wait_ge(mturned, 2 * NT)
            sp.dma_start(mix[:, :, :], x.rearrange("(t p) n -> p t n", p=P)).then_inc(xr_in, 16)
            sp.dma_start(rw[:, :, :], router_w[0].rearrange("(k p) e -> p k e", p=P)).then_inc(late_in, 16)
            for q in range(QUARTERS):
                raw_free(7, q)
                weights(7, q)
            sp.wait_ge(zero_set, 1)
            for i in range(PAD_ROWS // P):
                sp.dma_start(h2_d[T + i * P:T + (i + 1) * P, :], zero[:, :]).then_inc(pads_out, 16)
                sp.dma_start(acc_d[T + i * P:T + (i + 1) * P, :], zero[:, :]).then_inc(pads_out, 16)
            for t in range(NT):
                sp.wait_ge(x2_set, t + 1)
                sp.dma_start(acc_d[t * P:(t + 1) * P, :], mix[:, t, :]).then_inc(acc_out, 16)
                sp.wait_ge(h2_set, t + 1)
                sp.dma_start(h2_d[t * P:(t + 1) * P, :], h2[:, t % 2, :]).then_inc(h2_out[t % 2], 16)

            sp.wait_ge(jobs_set, 1)
            e0 = sp.value_load(jobt[0:1, 0, 0:1], min_val=0, max_val=NE - 1)
            for q in range(QUARTERS):
                raw_free(DENSE_UNITS, q)
                sp.dma_start(raw[:, q, :, :], expert_part(w1v, q, e0, slice(0, UNIT))).then_inc(raw_in[q], 16)
            sp.wait_ge(quarter_used, 4 * DENSE_UNITS)
            sp.dma_start(brow[:, 0:2 * FF].bitcast(F32), bias_part(e0, slice(0, 2 * FF))).then_inc(brow1_in, 16)
            def wait(semaphore, value):
                sp.wait_ge(semaphore, value)
                sp.sem_inc(sync_mark, 1)

            with sp.Fori(0, JOBS, 1) as j:
                left = sp.value_load(jobt[0:1, 2, bass.ds(j, 1)], min_val=0, max_val=T)
                with sp.If(left > 0):
                    e = sp.value_load(jobt[0:1, 0, bass.ds(j, 1)], min_val=0, max_val=NE - 1)
                    en = sp.value_load(jobt[0:1, 0, bass.ds(j + 1, 1)], min_val=0, max_val=NE - 1)
                    for c in range(1, JOB_UNITS + 1):
                        if c == 2:
                            wait(quarter_used, j * 24 + 4 * DENSE_UNITS)
                            sp.dma_start(brow[:, 2 * FF:BW].bitcast(F32),
                                         bias_part(e, slice(2 * FF, BW))).then_inc(brow2_in, 16)
                        if c == JOB_UNITS:
                            wait(quarter_used, j * 24 + 4 * (DENSE_UNITS + 4))
                            sp.dma_start(brow[:, 0:2 * FF].bitcast(F32),
                                         bias_part(en, slice(0, 2 * FF))).then_inc(brow1_in, 16)
                        for q in range(QUARTERS):
                            wait(split_hi, j * 24 + 4 * (DENSE_UNITS + c) + q - 3)
                            if q < 3:
                                wait(split_lo_dve, j * 18 + 3 * (DENSE_UNITS + c) + q - 2)
                            else:
                                wait(split_lo_pool, j * 6 + DENSE_UNITS + c)
                            if c < 4:
                                src = expert_part(w1v, q, e, slice(c * UNIT, (c + 1) * UNIT))
                            elif c < 6:
                                src = expert_part(w2v, q, e, slice((c - 4) * UNIT, (c - 3) * UNIT))
                            else:
                                src = expert_part(w1v, q, en, slice(0, UNIT))
                            sp.dma_start(raw[:, q, :, :], src).then_inc(raw_in[q], 16)
                    wait(brow1_in, j * 16 + 32)
                    wait(brow2_in, j * 16 + 16)
            sp.dma_start(g2row[:, :], final_g.rearrange("(a d) -> a d", a=1).broadcast_to([P, D])).then_inc(gfin_in, 16)
            sp.wait_ge(jobs_over, 1)
            for t in range(NT):
                sp.dma_start(mix[:, t, :], acc_d[t * P:(t + 1) * P, :]).then_inc(fin_in[t], 16)
            for t in range(NT):
                sp.wait_ge(fset, t + 1)
                sp.dma_start(out[t * P:(t + 1) * P, :], mix[:, t, :]).then_inc(fin_out, 16)
            sp.wait_ge(fin_out, 16 * NT)

        @block.tensor
        def _(pe):
            def mm3(o, sh, sl, mh_, ml_, start, stop, skip=False):
                pe.matmul(o, sh, mh_, start=start, stop=False, skip_group_check=skip)
                pe.matmul(o, sh, ml_, start=False, stop=False, skip_group_check=skip)
                return pe.matmul(o, sl, mh_, start=False, stop=stop, skip_group_check=skip)

            pe.wait_ge(const_set, 1)
            for t in range(NT):
                pe.wait_ge(normed, t + 1)
                for half in range(2):
                    i = 2 * t + half
                    if i >= 8:
                        pe.wait_ge(turned_lo, i - 7)
                    for k in range(4):
                        m = pe.transpose(ps[:, i % 8, k * P:(k + 1) * P],
                                         xs[:, t, (4 * half + k) * P:(4 * half + k + 1) * P], ident[:, :])
                    m.then_inc(turned, 1)

            def split_ready(n, q):
                pe.wait_ge(split_hi, 4 * n + q + 1)
                if q < 3:
                    pe.wait_ge(split_lo_dve, 3 * n + q + 1)
                else:
                    pe.wait_ge(split_lo_pool, n + 1)

            def unit(n, sth, stl):
                feature_major = n < 3
                for q in range(QUARTERS):
                    split_ready(n, q)
                    for c in range(CHAINS[n]):
                        if q == 0 and n >= 1 and c < CHAINS[n - 1]:
                            pe.wait_ge(*taken(n - 1, c))
                        if q == 0 and n == 4 and c >= CHAINS[3]:
                            pe.wait_ge(*taken(2, c))
                        first, last = q == 0, q == QUARTERS - 1
                        if feature_major or (n == 3 and c < 2):
                            for a in range(2):
                                k = 2 * q + a
                                f = 0 if n == 3 else c // 2
                                h_, l_ = (w[:, q, a, f * P:(f + 1) * P] for w in (whi, wlo))
                                half = c % 2
                                m = mm3(ps[:, c, :], h_, l_, sth[:, k, half * 512:half * 512 + 512],
                                        stl[:, k, half * 512:half * 512 + 512],
                                        first and a == 0, last and a == 1)
                        elif n == 3:
                            for t in range(4 * (c - 2), 4 * (c - 2) + 4):
                                o = ps[:, c, (t % 4) * P:(t % 4 + 1) * P]
                                if first:
                                    pe.matmul(o, ones2[:, :], brow[:, B_AV:B_AV + P], start=t % 4 == 0,
                                              stop=False, skip_group_check=True)
                                for a in range(2):
                                    k = 2 * q + a
                                    m = mm3(o, sth[:, k, t * P:(t + 1) * P], stl[:, k, t * P:(t + 1) * P],
                                            whi[:, q, a, P:2 * P], wlo[:, q, a, P:2 * P],
                                            False, last and a == 1, True)
                        else:
                            if first:
                                b = {4: B_HI, 5: B_HG, 6: B_OUT, 7: B_OUT + UNIT}[n]
                                pe.matmul(ps[:, c, :], ones2[:, :], brow[:, b:b + UNIT], start=True, stop=False)
                            for a in range(2):
                                k = 2 * q + a
                                m = mm3(ps[:, c, :], sth[:, k, c * P:(c + 1) * P], stl[:, k, c * P:(c + 1) * P],
                                        whi[:, q, a, :], wlo[:, q, a, :], False, last and a == 1)
                        if last and c < CHAINS[n] - 1:
                            m.then_inc(chain_done, 1)
                    m.then_inc(quarter_used, 1)

            pe.wait_ge(turned_lo, 2 * NT)
            for n in range(3):
                unit(n, th, tl)
            pe.wait_ge(brow_in, 16)
            for n in range(3, 6):
                unit(n, th, tl)

            pe.wait_ge(*taken(5, 7))

            def scores(b):
                n, kv = divmod(b, 2)
                if b >= 2:
                    pe.wait_ge(score_added, b - 1)
                lo = P if n == 0 else 0
                for i in range(GROUP):
                    m = pe.matmul(ps[:, 2 * kv + i // 2, (i % 2) * 256 + lo:(i % 2) * 256 + 256],
                                  aq[64 * kv:64 * kv + 64, i, n * P:(n + 1) * P],
                                  ak[64 * kv:64 * kv + 64, n * P + lo:n * P + 256],
                                  start=True, stop=True)
                m.then_inc(scored, 1)

            scores(0)
            for b in range(2 * NT):
                n, kv = divmod(b, 2)
                if b + 1 < 2 * NT:
                    scores(b + 1)
                pe.wait_ge(exped, b + 1)
                if b >= 1:
                    pe.wait_ge(pT_act, b)
                    pe.wait_ge(pT_dve, b)
                for half in range(2):
                    if n == 0 and half == 0:
                        pe.sem_inc(probs_turned, 1)
                        continue
                    for i in range(GROUP):
                        m = pe.transpose(ps[:, 4 + half, i * P:(i + 1) * P],
                                         score[:, kv, i, half * P:half * P + P], ident[:, :])
                    m.then_inc(probs_turned, 1)
                pe.wait_ge(pT_act, b + 1)
                pe.wait_ge(pT_dve, b + 1)
                if b >= 2:
                    pe.wait_ge(heads_out, b - 1)
                for i in range(GROUP):
                    o = ps[:, 6 + kv, i * HD:(i + 1) * HD]
                    if n > 0:
                        pe.matmul(o, probT[:, 0, i, :], av[:, n - 1, kv * HD:kv * HD + HD], start=True, stop=False)
                    m = pe.matmul(o, probT[:, 1, i, :], av[:, n, kv * HD:kv * HD + HD], start=n == 0, stop=True)
                m.then_inc(heads_done, 1)

            pe.wait_ge(heads_out, 2 * NT)
            for hd in range(HH):
                if hd == 0:
                    pe.wait_ge(keys_set, HH)
                else:
                    pe.wait_ge(rec_out, 2 * hd)
                for t in range(NT):
                    m = pe.matmul(ps[:, 2 + t // 4, (t % 4) * P:(t % 4 + 1) * P],
                                  hk[:, hd, t * P:(t + 1) * P], hq[:, hd, t * P:(t + 1) * P],
                                  start=True, stop=True)
                m.then_inc(diag_done, 1)
                for L in range(LEVELS):
                    s = STEPS * hd + L
                    lev = LEVELS * hd + L
                    h = 64 >> L
                    pe.wait_ge(prod_dve, dve_prods_by(s))
                    pe.wait_ge(prod_pool, pool_prods_by(s))
                    if lev >= 2:
                        pe.wait_ge(level_copied, lev - 1)
                    for t in range(NT):
                        v = hp[:, s % 2, t * P:(t + 1) * P]
                        m = pe.matmul(ps[:, lev % 2, t * 64:(t + 1) * 64], v,
                                      v.rearrange("p (m two h) -> p m two h", two=2, h=h)[:, :, 1, :],
                                      start=True, stop=True)
                    m.then_inc(level_used, 1)
                s = STEPS * hd + LEVELS
                pe.wait_ge(prod_pool, pool_prods_by(s))
                if hd > 0:
                    pe.wait_ge(kbT_set, 2 * hd)
                for t in range(NT):
                    m = pe.transpose(ps[:, 4 + t // 4, (t % 4) * P:(t % 4 + 1) * P],
                                     hp[:, s % 2, t * P:(t + 1) * P], ident[:, :])
                m.then_inc(level_used, 1)
                pe.wait_ge(kbT_set, 2 * hd + 2)
                if hd > 0:
                    pe.wait_ge(states_set, hd)
                for t in range(NT - 1):
                    m = pe.matmul(ps[:, 6 + t // 4, (t % 4) * P:(t % 4 + 1) * P], kbT[:, t, :],
                                  hv[:, t, hd * P:(hd + 1) * P], start=True, stop=True)
                m.then_inc(added_state, 1)
                s = STEPS * hd + LEVELS + 1
                pe.wait_ge(prod_dve, dve_prods_by(s))
                pe.wait_ge(level_copied, LEVELS * (hd + 1))
                pe.wait_ge(states_set, hd + 1)
                for t in range(NT):
                    o = ps[:, 2 + t // 4, (t % 4) * P:(t % 4 + 1) * P]
                    m = pe.matmul(o, attT[hd % 2][:, t, :], hv[:, t, hd * P:(hd + 1) * P],
                                  start=True, stop=t == 0)
                    if t > 0:
                        m = pe.matmul(o, hp[:, s % 2, t * P:(t + 1) * P], state[:, t - 1, :],
                                      start=False, stop=True)
                m.then_inc(level_used, 1)

            pe.wait_ge(rec_out, 2 * HH)
            for t in range(NT):
                pe.wait_ge(mnormed, t + 1)
                for half in range(2):
                    i = 2 * t + half
                    if i >= 8:
                        pe.wait_ge(mturned_lo, i - 7)
                    for k in range(4):
                        m = pe.transpose(ps[:, i % 8, k * P:(k + 1) * P],
                                         mix[:, t, (4 * half + k) * P:(4 * half + k + 1) * P], ident[:, :])
                    m.then_inc(mturned, 1)
            pe.wait_ge(mturned_lo, 2 * NT)
            unit(6, mh, ml)
            unit(7, mh, ml)

            pe.wait_ge(*taken(7, 7))
            pe.wait_ge(rw_lo, 1)
            pe.wait_ge(late_set, 1)
            for t in range(NT):
                pe.wait_ge(h2_set, t + 1)
                for half in range(2):
                    if t > 0:
                        pe.wait_ge(h2_lo, 2 * t - 1 + half)
                    for k in range(4):
                        m = pe.transpose(ps[:, half, k * P:(k + 1) * P],
                                         h2[:, t % 2, (4 * half + k) * P:(4 * half + k + 1) * P], ident[:, :])
                    m.then_inc(h2_turned, 1)
                if t > 0:
                    pe.wait_ge(top_set, t)
                for k in range(KT):
                    if k % 4 == 0:
                        pe.wait_ge(h2_lo, 2 * t + 1 + k // 4)
                    m = mm3(ps[:, 2, 0:NE], h2Th[:, k, :], h2Tl[:, k, :], rwh[:, k, :], rwl[:, k, :],
                            k == 0, k == KT - 1)
                m.then_inc(logits_done, 1)
                pe.wait_ge(picked_set, t + 1)
                pe.matmul(ps[:, 3, 0:NE], before[:, :], picked[:, :], start=True, stop=False)
                pe.matmul(ps[:, 3, 0:NE], onesf[:, :], count[:, t, :], start=False, stop=True).then_inc(ranked, 1)
            pe.wait_ge(pos_set, NT)
            pe.matmul(ps[0:NE, 4, 0:1], count[:, NT, :], onesf[:, 0:1], start=True, stop=True).then_inc(jn, 1)
            pe.wait_ge(jn_set, 1)
            pe.matmul(ps[0:NE, 5, 0:1], before[0:NE, 0:NE], nexp[:, 1:2], start=True, stop=True).then_inc(jbase, 1)
            pe.wait_ge(jrows, 1)
            pe.matmul(ps[0:1, 6, 0:3 * JT_W], onesf[0:NE, 0:1],
                      jobr[:, :, :].rearrange("p a b -> p (a b)"), start=True, stop=True).then_inc(jsum, 1)

            def x_turn(r):
                b, half = divmod(r, 2)
                for k in range(4):
                    m = pe.transpose(ps[:, 6 + half, k * P:(k + 1) * P],
                                     xg[:, b, (4 * half + k) * P:(4 * half + k + 1) * P], ident[:, :])
                m.then_inc(x_turned, 1)

            pe.wait_ge(jobs_set, 1)
            pe.wait_ge(gathered, 32)
            for r in range(4):
                if r >= 2:
                    pe.wait_ge(xT_lo, r - 1)
                x_turn(r)

            def job(j, two):
                def a_turn(c):
                    for b in range(2):
                        pe.wait_ge(act_set, j * 8 + 2 * c + b + 1)
                        pe.wait_ge(aT_lo, j * 8 + 2 * c + b + 1)
                        if b == 1 and not two:
                            pe.sem_inc(a_turned[1], 1)
                            continue
                        for k in range(2):
                            m = pe.transpose(ps[:, 4 + b, k * P:(k + 1) * P], glu[:, b, k * P:(k + 1) * P],
                                             ident[:, :])
                        m.then_inc(a_turned[b], 1)

                for c in range(JOB_UNITS):
                    sh, sl = (xTh, xTl) if c < 4 else (aTh, aTl)
                    bias = c * UNIT if c < 4 else 2 * FF + (c - 4) * UNIT
                    if c == 0:
                        pe.wait_ge(xT_hi, j * 4 + 4)
                        pe.wait_ge(xT_lo, j * 4 + 4)
                        pe.wait_ge(brow1_in, j * 16 + 16)
                    if c == 4:
                        pe.wait_ge(aT_hi, j * 8 + 8)
                        pe.wait_ge(aT_lo, j * 8 + 8 + 2)
                        pe.wait_ge(brow2_in, j * 16 + 16)
                    if c < 2:
                        pe.wait_ge(y_set, j * 4 + 2 * c + 2)
                    else:
                        pe.wait_ge(hid_taken, j * 8 + 2 * c - 2)
                    for q in range(QUARTERS):
                        pe.wait_ge(split_hi, j * 24 + 4 * (DENSE_UNITS + c) + q + 1)
                        if q < 3:
                            pe.wait_ge(split_lo_dve, j * 18 + 3 * (DENSE_UNITS + c) + q + 1)
                        else:
                            pe.wait_ge(split_lo_pool, j * 6 + DENSE_UNITS + c + 1)
                        for b in range(2 if two else 1):
                            o = ps[:, 2 * b + c % 2, :]
                            if q == 0:
                                pe.matmul(o, ones2[:, :], brow[:, bias:bias + UNIT], start=True, stop=False)
                            for a in range(2):
                                k = 2 * q + a
                                m = mm3(o, sh[:, k, b, :], sl[:, k, b, :], whi[:, q, a, :], wlo[:, q, a, :],
                                        False, q == QUARTERS - 1 and a == 1)
                        m.then_inc(quarter_used, 1)
                    if 1 <= c <= 2:
                        a_turn(c - 1)
                    if c == 3:
                        a_turn(2)
                        pe.wait_ge(gathered, j * 32 + 64)
                        for r in range(4):
                            pe.wait_ge(xT_lo, j * 4 + 3 + r)
                            x_turn(r)
                        a_turn(3)

            pe.sem_inc(a_turned[0], 1)
            pe.sem_inc(a_turned[1], 1)
            with pe.Fori(0, JOBS, 1) as j:
                left = pe.value_load(jobt[0:1, 2, bass.ds(j, 1)], min_val=0, max_val=T)
                with pe.If(left > P):
                    job(j, True)
                with pe.If(left < P + 1):
                    with pe.If(left > 0):
                        job(j, False)

        @block.scalar
        def _(act):
            def split(n, q):
                act.wait_ge(raw_in[q], 16 * (n + 1 + 3 * (n >= 2)))
                if n > 0:
                    act.wait_ge(quarter_used, 4 * n + q - 3)
                cols = 256 if n == 3 else UNIT
                act.activation(whi[:, q, :, 0:cols], raw[:, q, :, 0:cols], ACT.Copy).then_inc(split_hi, 1)

            def root(o, i, n):
                act.activation(o, i, ACT.Sqrt, scale=1.0 / n, bias=epsc[:, 0:1]).then_inc(rooted, 1)

            act.wait_ge(eps_set, 1)
            for t in range(NT + 1):
                if t < NT:
                    act.wait_ge(x_in[t], 16)
                    if t > 0:
                        act.wait_ge(squared, t)
                    act.activation(junk0[:, :], xs[:, t, :], ACT.Square, accum_out=ss[:, t:t + 1]).then_inc(squared, 1)
                    act.wait_ge(squared, t + 1)
                    root(rstd[:, t:t + 1], ss[:, t:t + 1], D)
                if t == 1:
                    act.wait_ge(lb_max, 1)
                    act.activation(lbe[:, :, :], lbe[:, :, :], ACT.Exp).then_inc(lb_exp, 1)
                if 2 <= t <= 5:
                    split(0, t - 2)
                if t >= 1:
                    for half in range(2):
                        i = 2 * (t - 1) + half
                        act.wait_ge(turned, i + 1)
                        act.activation(th[:, 4 * half:4 * half + 4, (t - 1) * P:t * P],
                                       ps[:, i % 8, :].rearrange("p (k n) -> p k n", k=4),
                                       ACT.Copy).then_inc(turned_hi, 1)
            act.wait_ge(bias_in, 16 * 5)
            act.activation(bph[:, :], bp[:, :], ACT.Copy).then_inc(bias_hi, 1)

            for n in range(6):
                for q in range(3):
                    split(n + 1, q)
                for c in range(CHAINS[n]):
                    chain_ready(act, n, c)
                    cols = slice((c % 2) * 512, (c % 2) * 512 + 512)
                    if n == 0:
                        act.activation(hf[:, c // 2, cols], ps[:, c, :], ACT.Sigmoid,
                                       bias=bcol[:, 9 + c // 2:10 + c // 2]).then_inc(taken_act, 1)
                    elif n == 1:
                        act.activation(hq[:, c // 2, cols], ps[:, c, :], ACT.Sigmoid,
                                       bias=bcol[:, 5 + c // 2:6 + c // 2]).then_inc(taken_act, 1)
                    elif n == 3 and c >= 2:
                        act.wait_ge(tinit_out, 16)
                        act.activation(av[:, 4 * (c - 2):4 * (c - 2) + 4, :],
                                       ps[:, c, :].rearrange("p (t n) -> p t n", t=4),
                                       ACT.Copy).then_inc(taken_act, 1)
                    elif n == 4:
                        act.activation(hv[:, c, :], ps[:, c, :], ACT.Copy).then_inc(taken_act, 1)
                    elif n == 5:
                        if c >= 2:
                            act.wait_ge(hg_out[c % 2], 16 * (c // 2))
                        act.activation(hgs[:, c % 2, :], ps[:, c, :], ACT.Sigmoid).then_inc(taken_act, 1)
                split(n + 1, 3)

            def exps(b):
                kv = b % 2
                act.wait_ge(maxed, b + 1)
                lo = P if b < 2 else 0
                for i in range(GROUP):
                    m = act.activation(score[:, kv, i, lo:], score[:, kv, i, lo:], ACT.Exp,
                                       bias=stat[:, 1, b, i:i + 1], accum_out=stat[:, 3, b, i:i + 1])
                m.then_inc(exped, 1)
                act.activation(stat[:, 4, b, :], stat[:, 2, b, :], ACT.Exp).then_inc(sinked, 1)

            exps(0)
            for b in range(2 * NT):
                if b + 1 < 2 * NT:
                    exps(b + 1)
                if b < 2:
                    act.sem_inc(pT_act, 1)
                else:
                    act.wait_ge(probs_turned, 2 * b + 1)
                    act.wait_ge(heads_done, b)
                    act.activation(probT[:, 0, :, :], ps[:, 4, :].rearrange("p (i n) -> p i n", i=GROUP),
                                   ACT.Copy).then_inc(pT_act, 1)

            for hd in range(HH):
                act.wait_ge(keys_set, hd + 1)
                act.activation(hf[:, hd, :], hf[:, hd, :], ACT.Ln).then_inc(logs_set, 1)

            def outs(hd):
                act.wait_ge(level_used, STEPS * (hd + 1))
                for i in range(2):
                    act.activation(mix[:, 4 * i:4 * i + 4, ATTN_W + hd * P:ATTN_W + (hd + 1) * P],
                                   ps[:, 2 + i, :].rearrange("p (t n) -> p t n", t=4),
                                   ACT.Copy).then_inc(rec_out, 1)

            for s in range(STEPS * HH):
                hd, L = divmod(s, STEPS)
                if L < LEVELS + 1:
                    act.wait_ge(arg_set, args_by(s))
                    act.activation(he[:, s % 2, :], he[:, s % 2, :], ACT.Exp).then_inc(exp_set, 1)
                else:
                    act.wait_ge(prod_dve, dve_prods_by(s - 2))
                    act.wait_ge(prod_pool, pool_prods_by(s - 2))
                    act.activation(he[:, s % 2, :], hf[:, hd, :], ACT.Exp).then_inc(exp_set, 1)
                    act.wait_ge(level_used, STEPS * hd + LEVELS + 1)
                    if hd > 0:
                        act.wait_ge(added_state, hd)
                    for i in range(2):
                        act.activation(kbT[:, 4 * i:4 * i + 4, :],
                                       ps[:, 4 + i, :].rearrange("p (t n) -> p t n", t=4),
                                       ACT.Copy).then_inc(kbT_set, 1)
                if L == 1 and hd > 0:
                    outs(hd - 1)
            outs(HH - 1)

            k = 0
            act.wait_ge(rec_out, 2 * HH)
            act.wait_ge(level_used, STEPS * HH)
            for t in range(NT):
                for g in range(5):
                    cols = slice(0, ATTN_W) if g == 0 else slice(ATTN_W + (g - 1) * P, ATTN_W + g * P)
                    if k > 0:
                        act.wait_ge(msq, k)
                    act.activation(junk[:, 0:cols.stop - cols.start], mix[:, t, cols], ACT.Square,
                                   accum_out=ssa[:, t, g:g + 1]).then_inc(msq, 1)
                    k += 1
            act.wait_ge(msq, 5 * NT)
            root(rsa[:, :, 0], ssa[:, :, 0], ATTN_W)
            root(rsa[:, :, 1:], ssa[:, :, 1:], P)
            for i in range(2 * NT):
                t, half = divmod(i, 2)
                act.wait_ge(mturned, i + 1)
                act.activation(mh[:, 4 * half:4 * half + 4, t * P:(t + 1) * P],
                               ps[:, i % 8, :].rearrange("p (k n) -> p k n", k=4),
                               ACT.Copy).then_inc(mturned_hi, 1)
            for q in range(3):
                split(7, q)
            split(7, 3)
            act.wait_ge(late_in, 48)
            act.activation(rwh[:, :, :], rw[:, :, :], ACT.Copy).then_inc(rw_hi, 1)

            def gate(t):
                act.wait_ge(top_set, t + 1)
                act.activation(gexp[:, :], top[:, 0:TOPK], ACT.Exp, bias=ntop[:, 0:1],
                               accum_out=gden[:, 0:1]).then_inc(gate_exp, 1)

            for t in range(NT):
                act.wait_ge(x2_set, t + 1)
                if t > 0:
                    act.wait_ge(sq2, t)
                act.activation(junk[:, :], mix[:, t, :], ACT.Square, accum_out=ss[:, t:t + 1]).then_inc(sq2, 1)
                act.wait_ge(sq2, t + 1)
                root(rstd[:, t:t + 1], ss[:, t:t + 1], D)
            for t in range(NT):
                for half in range(2):
                    act.wait_ge(h2_turned, 2 * t + half + 1)
                    if t > 0 and half == 0:
                        act.wait_ge(logits_done, t)
                    act.activation(h2Th[:, 4 * half:4 * half + 4, :],
                                   ps[:, half, :].rearrange("p (k n) -> p k n", k=4),
                                   ACT.Copy).then_inc(h2_hi, 1)
                gate(t)

            def jsplit(j, c, q):
                act.wait_ge(raw_in[q], j * 96 + 16 * (DENSE_UNITS + c + 4))
                act.wait_ge(quarter_used, j * 24 + 4 * (DENSE_UNITS + c) + q - 3)
                act.activation(whi[:, q, :, :], raw[:, q, :, :], ACT.Copy).then_inc(split_hi, 1)

            def xT(j, r):
                b, half = divmod(r, 2)
                act.wait_ge(x_turned, j * 4 + r + 1)
                act.activation(xTh[:, 4 * half:4 * half + 4, b, :],
                               ps[:, 6 + half, :].rearrange("p (k n) -> p k n", k=4),
                               ACT.Copy).then_inc(xT_hi, 1)

            def sigmoid(j, c, b):
                act.wait_ge(glu_set, j * 8 + 2 * c + b + 1)
                act.activation(sig[:, b, :], glu[:, b, :], ACT.Sigmoid, scale=ALPHA).then_inc(sig_set, 1)

            def aT(j, c, b):
                act.wait_ge(a_turned[b], j * 4 + c + 2)
                act.activation(aTh[:, 2 * c:2 * c + 2, b, :],
                               ps[:, 4 + b, 0:256].rearrange("p (k n) -> p k n", k=2),
                               ACT.Copy).then_inc(aT_hi, 1)

            def y_out(j, c, b):
                act.wait_ge(quarter_used, j * 24 + 4 * (DENSE_UNITS + c) + 4)
                if c == 4 and b == 0:
                    act.wait_ge(tcur_set, j + 1)
                act.activation(y[:, b, (c - 4) * UNIT:(c - 3) * UNIT], ps[:, 2 * b + c % 2, :], ACT.Copy,
                               scale=gcur[:, b:b + 1]).then_inc(y_set, 1)

            act.wait_ge(jobs_set, 1)
            for q in range(QUARTERS):
                jsplit(0, 0, q)
            for r in range(4):
                xT(0, r)
            act.sem_inc(y_set, 4)
            with act.Fori(0, JOBS, 1) as j:
                left = act.value_load(jobt[0:1, 2, bass.ds(j, 1)], min_val=0, max_val=T)
                with act.If(left > 0):
                    for c in range(JOB_UNITS):
                        if 2 <= c <= 3:
                            aT(j, c - 2, 0)
                            aT(j, c - 2, 1)
                        jsplit(j, c + 1, 0)
                        jsplit(j, c + 1, 1)
                        if 1 <= c <= 3:
                            sigmoid(j, c - 1, 0)
                        if c == 5:
                            y_out(j, 4, 0)
                        jsplit(j, c + 1, 2)
                        if 1 <= c <= 3:
                            sigmoid(j, c - 1, 1)
                        if c == 5:
                            y_out(j, 4, 1)
                        jsplit(j, c + 1, 3)
                        if c == 3:
                            sigmoid(j, 3, 0)
                            sigmoid(j, 3, 1)
                            aT(j, 2, 0)
                            aT(j, 2, 1)
                            for r in range(4):
                                xT(j + 1, r)
                            aT(j, 3, 0)
                            aT(j, 3, 1)
                        if c == 5:
                            y_out(j, 5, 0)
                            y_out(j, 5, 1)

            for t in range(NT):
                act.wait_ge(fin_in[t], 16)
                if t > 0:
                    act.wait_ge(fsq, t)
                act.activation(junk[:, :], mix[:, t, :], ACT.Square, accum_out=ss[:, t:t + 1]).then_inc(fsq, 1)
                act.wait_ge(fsq, t + 1)
                root(rstd[:, t:t + 1], ss[:, t:t + 1], D)

        @block.vector
        def _(dve):
            steps = [0]

            def link(ins):
                steps[0] += 1
                ins.then_inc(dve_step, 1)
                dve.wait_ge(dve_step, steps[0])

            def invert(o, roots):
                dve.wait_ge(rooted, roots)
                link(dve.reciprocal(o, o))

            def split(n, q):
                cols = 256 if n == 3 else UNIT
                dve.wait_ge(split_hi, 4 * n + q + 1)
                dve.tensor_tensor(wlo[:, q, :, 0:cols], raw[:, q, :, 0:cols], whi[:, q, :, 0:cols].bitcast(F32),
                                  ALU.subtract).then_inc(split_lo_dve, 1)

            dve.memset(bp[:, :], 0.0).then_inc(bp_zero, 1)

            dve.wait_ge(const_in, 16 * N_CONST)
            for t in range(NT + 1):
                if t < NT:
                    invert(rstd[:, t:t + 1], t + 1)
                    dve.scalar_tensor_tensor(out=xs[:, t, :], in0=xs[:, t, :], scalar=rstd[:, t:t + 1],
                                             in1=grow[:, :], op0=ALU.mult, op1=ALU.mult).then_inc(normed, 1)
                if t == 0:
                    link(dve.tensor_tensor(lbm[:, :], lbl[:, 0, :], lbl[:, 1, :], ALU.max))
                    dve.tensor_tensor(lbe[:, 0, :], lbl[:, 0, :], lbm[:, :], ALU.subtract)
                    dve.tensor_tensor(lbe[:, 1, :], lbl[:, 1, :], lbm[:, :], ALU.subtract).then_inc(lb_max, 1)
                if t == 2:
                    dve.wait_ge(lb_exp, 1)
                    link(dve.tensor_tensor(lbm[:, :], lbe[:, 0, :], lbe[:, 1, :], ALU.add))
                    link(dve.reciprocal(lbm[:, :], lbm[:, :]))
                    link(dve.tensor_tensor(lb[:, :], lbe[:, 0, :], lbm[:, :], ALU.mult))
                    link(dve.tensor_scalar(oml[:, :], lb[:, :], -1.0, 1.0, ALU.mult, ALU.add))
                if 3 <= t <= 5:
                    split(0, t - 3)
                if t >= 1:
                    for half in range(2):
                        i = 2 * (t - 1) + half
                        dve.wait_ge(turned_hi, i + 1)
                        hi = th[:, 4 * half:4 * half + 4, (t - 1) * P:t * P].bitcast(F32)
                        dve.tensor_tensor(tl[:, 4 * half:4 * half + 4, (t - 1) * P:t * P],
                                          ps[:, i % 8, :].rearrange("p (k n) -> p k n", k=4), hi,
                                          ALU.subtract).then_inc(turned_lo, 1)

            for n in range(6):
                for q in range(3):
                    split(n + 1, q)
                for c in range(CHAINS[n]):
                    chain_ready(dve, n, c)
                    cols = slice((c % 2) * 512, (c % 2) * 512 + 512)
                    if n == 1:
                        dve.wait_ge(taken_act, sum(BY_ACT[:n]) + c + 1)
                        dve.scalar_tensor_tensor(out=hq[:, c // 2, cols], in0=ps[:, c, :],
                                                 scalar=bcol[:, 5 + c // 2:6 + c // 2], in1=hq[:, c // 2, cols],
                                                 op0=ALU.add, op1=ALU.mult).then_inc(taken_dve, 1)
                    elif n == 2:
                        dve.wait_ge(bias_out, 32)
                        dve.tensor_scalar(aq[:, c // 2, cols], ps[:, c, :], bcol[:, c // 2:c // 2 + 1],
                                          HD ** -0.5, ALU.add, ALU.mult).then_inc(taken_dve, 1)
                    elif n == 3 and c < 2:
                        dve.wait_ge(tinit_out, 16)
                        dve.tensor_scalar(ak[:, P + c * 512:P + c * 512 + 512], ps[:, c, :], bcol[:, 4:5],
                                          None, ALU.add).then_inc(taken_dve, 1)
                    elif n == 5:
                        dve.wait_ge(taken_act, sum(BY_ACT[:n]) + c + 1)
                        dve.tensor_tensor(hgs[:, c % 2, :], ps[:, c, :], hgs[:, c % 2, :],
                                          ALU.mult).then_inc(taken_dve, 1)

            dve.wait_ge(quarter_used, 4 * 6)
            dve.wait_ge(const_set, 2)
            for h in range(NQ):
                link(dve.scalar_tensor_tensor(out=alibi[:, h, :], in0=dist[:, :], scalar=-SLOPES[h],
                                              in1=closed[:, :], op0=ALU.mult, op1=ALU.add))

            def add_bias(b):
                n, kv = divmod(b, 2)
                dve.wait_ge(scored, b + 1)
                if b >= 2:
                    dve.wait_ge(probs_turned, 2 * b - 2)
                lo = P if n == 0 else 0
                s = score[:, kv, :, lo:]
                link(dve.tensor_tensor(s, ps[:, 2 * kv:2 * kv + 2, :].rearrange("p a (i k) -> p (a i) k", i=2)[:, :, lo:],
                                       alibi[:, GROUP * kv:GROUP * kv + GROUP, lo:], ALU.add))
                dve.sem_inc(score_added, 1)
                link(dve.tensor_reduce(stat[:, 0, b, :], s, AX, ALU.max))
                link(dve.tensor_tensor(stat[:, 0, b, :], stat[:, 0, b, :], sinks[:, GROUP * kv:GROUP * kv + GROUP], ALU.max))
                dve.tensor_scalar(stat[:, 1, b, :], stat[:, 0, b, :], -1.0, None, ALU.mult)
                link(dve.tensor_tensor(stat[:, 2, b, :], sinks[:, GROUP * kv:GROUP * kv + GROUP], stat[:, 0, b, :], ALU.subtract))
                dve.sem_inc(maxed, 1)

            add_bias(0)
            for b in range(2 * NT):
                n, kv = divmod(b, 2)
                if b + 1 < 2 * NT:
                    add_bias(b + 1)
                dve.wait_ge(exped, b + 1)
                dve.wait_ge(sinked, b + 1)
                link(dve.tensor_tensor(stat[:, 3, b, :], stat[:, 3, b, :], stat[:, 4, b, :], ALU.add))
                link(dve.reciprocal(stat[:, 5, b, :], stat[:, 3, b, :]))
                dve.wait_ge(probs_turned, 2 * b + 2)
                if b >= 1:
                    dve.wait_ge(heads_done, b)
                dve.tensor_copy(probT[:, 1, :, :], ps[:, 5, :].rearrange("p (i n) -> p i n", i=GROUP)).then_inc(pT_dve, 1)
                dve.wait_ge(heads_done, b + 1)
                dve.tensor_tensor(mix[:, n, kv * 256:kv * 256 + 256].rearrange("p (i d) -> p i d", i=GROUP),
                                  ps[:, 6 + kv, 0:256].rearrange("p (i d) -> p i d", i=GROUP),
                                  stat[:, 5, b, :].unsqueeze(2).broadcast_to([P, GROUP, HD]),
                                  ALU.mult).then_inc(heads_out, 1)

            for hd in range(HH):
                link(dve.tensor_scalar(hf[:, hd, :], hf[:, hd, :], oml[:, hd:hd + 1], lb[:, hd:hd + 1], ALU.mult, ALU.add))
                dve.tensor_scalar(hk[:, hd, :], hf[:, hd, :], -1.0, 1.0, ALU.mult, ALU.add).then_inc(keys_set, 1)
            dve.wait_ge(reset_set, 1)
            for hd in range(HH):
                dve.wait_ge(logs_set, hd + 1)
                dve.tensor_tensor_scan(hf[:, hd, :], reset[:, :], hf[:, hd, :], 0.0, ALU.mult, ALU.add).then_inc(sums_set, 1)
            dve.wait_ge(sums_set, HH)

            def args(s):
                hd, L = divmod(s, STEPS)
                e = he[:, s % 2, :]
                b = hf[:, hd, :]
                if s >= 2:
                    dve.wait_ge(prod_pool, pool_prods_by(s - 2))
                    dve.wait_ge(prod_dve, dve_prods_by(s - 2))
                if L < LEVELS:
                    h = 64 >> L
                    bv, ev = (z.rearrange("p (m two h) -> p m two h", two=2, h=h) for z in (b, e))
                    mid = bv[:, :, 0, h - 1:h].broadcast_to([P, T // (2 * h), h])
                    dve.tensor_tensor(ev[:, :, 1, :], bv[:, :, 1, :], mid, ALU.subtract)
                    dve.tensor_tensor(ev[:, :, 0, :], mid, bv[:, :, 0, :], ALU.subtract).then_inc(arg_set, 1)
                elif L == LEVELS:
                    bv, ev = (z.rearrange("p (t n) -> p t n", n=P) for z in (b, e))
                    dve.tensor_tensor(ev, bv[:, :, P - 1:P].broadcast_to([P, NT, P]), bv, ALU.subtract).then_inc(arg_set, 1)

            def prods(s):
                hd, L = divmod(s, STEPS)
                dve.wait_ge(exp_set, s + 1)
                if s >= 2:
                    dve.wait_ge(level_used, s - 1)
                if L < LEVELS:
                    h = 64 >> L
                    ov, qv, ev = (z.rearrange("p (m two h) -> p m two h", two=2, h=h)[:, :, 1, :]
                                  for z in (hp[:, s % 2, :], hq[:, hd, :], he[:, s % 2, :]))
                    dve.tensor_tensor(ov, qv, ev, ALU.mult).then_inc(prod_dve, 1)
                elif L == LEVELS + 1:
                    dve.tensor_copy(decay[:, :], he[:, s % 2, :].rearrange("p (t n) -> p t n", n=P)[:, :, P - 1])
                    link(dve.tensor_tensor(hp[:, s % 2, :], hq[:, hd, :], he[:, s % 2, :], ALU.mult))
                    dve.sem_inc(prod_dve, 1)

            def copies(s):
                hd, L = divmod(s, STEPS)
                a = attT[hd % 2]
                if L < LEVELS:
                    lev = LEVELS * hd + L
                    h = 64 >> L
                    if L == 0:
                        dve.wait_ge(diag_done, hd + 1)
                        link(dve.tensor_tensor(a[:, :, :], ps[:, 2:4, :].rearrange("p a (t n) -> p (a t) n", n=P),
                                               ident[:, :].unsqueeze(1).broadcast_to([P, NT, P]), ALU.mult))
                    dve.wait_ge(level_used, s + 1)
                    nb = 64 // h
                    link(dve.copy_predicated(
                        a[:, :, :].rearrange("p t (m two h) -> p t m two h", two=2, h=h)[:, :, :, 1, :],
                        maskL[:, L, :].rearrange("p (m h) -> p m h", h=h).unsqueeze(1).broadcast_to([P, NT, nb, h]),
                        ps[:, lev % 2, :].rearrange("p (t m h) -> p t m h", t=NT, h=h)))
                    dve.sem_inc(level_copied, 1)
                elif L == LEVELS + 1:
                    dve.wait_ge(added_state, hd + 1)
                    if hd > 0:
                        dve.wait_ge(level_used, STEPS * hd)
                    link(dve.tensor_copy(state[:, 0, :], ps[:, 6, 0:P]))
                    for t in range(1, NT - 1):
                        link(dve.scalar_tensor_tensor(out=state[:, t, :], in0=state[:, t - 1, :], scalar=decay[:, t:t + 1],
                                                      in1=ps[:, 6 + t // 4, (t % 4) * P:(t % 4 + 1) * P],
                                                      op0=ALU.mult, op1=ALU.add))
                    dve.sem_inc(states_set, 1)

            for s in range(STEPS * HH + 2):
                if s < STEPS * HH:
                    args(s)
                if 1 <= s <= STEPS * HH:
                    prods(s - 1)
                if s >= 2:
                    copies(s - 2)

            invert(rsa[:, :, :], NT + 2)
            dve.wait_ge(gmix_in, 32)
            dve.wait_ge(hgt_set, 1)
            for t in range(NT + 1):
                if t < NT:
                    o = mix[:, t, ATTN_W:]
                    link(dve.tensor_tensor(o.rearrange("p (h n) -> p h n", h=HH), o.rearrange("p (h n) -> p h n", h=HH),
                                           rsa[:, t, 1:].unsqueeze(2).broadcast_to([P, HH, P]), ALU.mult))
                    dve.tensor_tensor(o, o, hgt[:, t, :], ALU.mult)
                    link(dve.scalar_tensor_tensor(out=mix[:, t, 0:ATTN_W], in0=mix[:, t, 0:ATTN_W], scalar=rsa[:, t, 0:1],
                                                  in1=grow[:, 0:ATTN_W], op0=ALU.mult, op1=ALU.mult))
                    dve.sem_inc(mnormed, 1)
                if t >= 1:
                    for half in range(2):
                        i = 2 * (t - 1) + half
                        dve.wait_ge(mturned_hi, i + 1)
                        dve.tensor_tensor(ml[:, 4 * half:4 * half + 4, (t - 1) * P:t * P],
                                          ps[:, i % 8, :].rearrange("p (k n) -> p k n", k=4),
                                          mh[:, 4 * half:4 * half + 4, (t - 1) * P:t * P].bitcast(F32),
                                          ALU.subtract).then_inc(mturned_lo, 1)
            for q in range(3):
                split(7, q)
            dve.wait_ge(xr_in, 16)
            for c in range(8):
                chain_ready(dve, 6, c)
                dve.tensor_tensor(mix[:, c, 0:UNIT], mix[:, c, 0:UNIT], ps[:, c, :], ALU.add).then_inc(taken_dve, 1)
            dve.wait_ge(rw_hi, 1)
            dve.tensor_tensor(rwl[:, :, :], rw[:, :, :], rwh[:, :, :].bitcast(F32), ALU.subtract).then_inc(rw_lo, 1)
            dve.wait_ge(late_set, 1)
            link(dve.memset(count[:, 0, :], 0.0))
            for c in range(8):
                chain_ready(dve, 7, c)
                link(dve.tensor_tensor(mix[:, c, UNIT:], mix[:, c, UNIT:], ps[:, c, :], ALU.add))
                dve.sem_inc(taken_dve, 1)
                dve.sem_inc(x2_set, 1)

            for t in range(NT):
                invert(rstd[:, t:t + 1], NT + 2 + t + 1)
                if t >= 2:
                    dve.wait_ge(h2_out[t % 2], 16 * (t // 2))
                dve.scalar_tensor_tensor(out=h2[:, t % 2, :], in0=mix[:, t, :], scalar=rstd[:, t:t + 1],
                                         in1=g2row[:, :], op0=ALU.mult, op1=ALU.mult).then_inc(h2_set, 1)
                for half in range(2):
                    dve.wait_ge(h2_hi, 2 * t + half + 1)
                    dve.tensor_tensor(h2Tl[:, 4 * half:4 * half + 4, :],
                                      ps[:, half, :].rearrange("p (k n) -> p k n", k=4),
                                      h2Th[:, 4 * half:4 * half + 4, :].bitcast(F32), ALU.subtract).then_inc(h2_lo, 1)
                dve.wait_ge(logits_done, t + 1)
                if t > 0:
                    dve.wait_ge(gate_exp, t)
                link(dve.tensor_tensor(logit[:, :], ps[:, 2, 0:NE], rb[:, :], ALU.add))
                link(dve.max(top[:, :], logit[:, :]))
                dve.max_index(topi[:, :], top[:, :], logit[:, :])
                link(dve.tensor_scalar(ntop[:, :], top[:, 0:1], -1.0, None, ALU.mult))
                dve.sem_inc(top_set, 1)
                link(dve.tensor_copy(topf[:, :], topi[:, :]))
                link(dve.tensor_tensor(hot[:, :, :], iotaE[:, :].unsqueeze(1).broadcast_to([P, TOPK, NE]),
                                       topf[:, 0:TOPK].unsqueeze(2).broadcast_to([P, TOPK, NE]), ALU.is_equal))
                link(dve.tensor_reduce(picked[:, :], hot[:, :, :].rearrange("p k e -> p e k"), AX, ALU.add))
                dve.sem_inc(picked_set, 1)
                link(dve.tensor_tensor(count[:, t + 1, :], count[:, t, :], picked[:, :], ALU.add))
                dve.wait_ge(ranked, t + 1)
                link(dve.tensor_tensor(hot[:, :, :], hot[:, :, :],
                                       ps[:, 3, 0:NE].unsqueeze(1).broadcast_to([P, TOPK, NE]), ALU.mult))
                link(dve.tensor_reduce(rank[:, :], hot[:, :, :], AX, ALU.add))
                link(dve.scalar_tensor_tensor(out=pos[:, t, :], in0=topf[:, 0:TOPK], scalar=float(T), in1=rank[:, :],
                                              op0=ALU.mult, op1=ALU.add))
                dve.wait_ge(gate_exp, t + 1)
                link(dve.reciprocal(grec[:, :], gden[:, :]))
                dve.tensor_scalar(load[:, t, :, 1], gexp[:, :], grec[:, 0:1], None, ALU.mult)
                link(dve.tensor_copy(load[:, t, :, 0], tok[:, t:t + 1].broadcast_to([P, TOPK])))
                dve.sem_inc(pos_set, 1)

            dve.wait_ge(jn, 1)
            link(dve.tensor_copy(nexp[:, 0:1], ps[0:NE, 4, 0:1]))
            link(dve.tensor_scalar(nexp[:, 1:2], nexp[:, 0:1], 0.0, None, ALU.is_gt))
            for k in range(1, T // JOB_T):
                link(dve.scalar_tensor_tensor(out=nexp[:, 1:2], in0=nexp[:, 0:1], scalar=float(k * JOB_T), in1=nexp[:, 1:2],
                                              op0=ALU.is_gt, op1=ALU.add))
            dve.sem_inc(jn_set, 1)
            dve.wait_ge(jbase, 1)
            link(dve.tensor_copy(nexp[:, 2:3], ps[0:NE, 5, 0:1]))
            link(dve.tensor_scalar(jobm[:, 0, :], jobi[:, :], nexp[:, 2:3], None, ALU.subtract))
            link(dve.tensor_scalar(jobm[:, 1, :], jobm[:, 0, :], 0.0, None, ALU.is_ge))
            link(dve.scalar_tensor_tensor(out=jobm[:, 1, :], in0=jobm[:, 0, :], scalar=nexp[:, 1:2], in1=jobm[:, 1, :],
                                          op0=ALU.is_lt, op1=ALU.mult))
            dve.tensor_scalar(jobr[:, 0, :], jobm[:, 1, :], eid[:, 0:1], None, ALU.mult)
            link(dve.tensor_scalar(nexp[:, 3:4], eid[:, 0:1], float(T // JOB_T), None, ALU.mult))
            dve.scalar_tensor_tensor(out=jobr[:, 1, :], in0=jobm[:, 0, :], scalar=nexp[:, 3:4], in1=jobm[:, 1, :],
                                     op0=ALU.add, op1=ALU.mult)
            link(dve.tensor_scalar(jobr[:, 2, :], jobm[:, 0, :], -float(JOB_T), nexp[:, 0:1], ALU.mult, ALU.add))
            link(dve.tensor_tensor(jobr[:, 2, :], jobr[:, 2, :], jobm[:, 1, :], ALU.mult))
            dve.sem_inc(jrows, 1)
            dve.wait_ge(jsum, 1)
            dve.tensor_copy(jobt[:, :, :].rearrange("p a b -> p (a b)"), ps[0:1, 6, 0:3 * JT_W]).then_inc(jobs_set, 1)
            dve.wait_ge(jobs_set, 1)

            def jsplit(j, c, q):
                dve.wait_ge(split_hi, j * 24 + 4 * (DENSE_UNITS + c) + q + 1)
                dve.tensor_tensor(wlo[:, q, :, :], raw[:, q, :, :], whi[:, q, :, :].bitcast(F32),
                                  ALU.subtract).then_inc(split_lo_dve, 1)

            def xT(j, r):
                b, half = divmod(r, 2)
                dve.wait_ge(xT_hi, j * 4 + r + 1)
                k = slice(4 * half, 4 * half + 4)
                dve.tensor_tensor(xTl[:, k, b, :], ps[:, 6 + half, :].rearrange("p (k n) -> p k n", k=4),
                                  xTh[:, k, b, :].bitcast(F32), ALU.subtract).then_inc(xT_lo, 1)

            def hidden(j, c, b):
                hid = ps[:, 2 * b + c % 2, :].rearrange("p (n two) -> p n two", two=2)
                dve.wait_ge(quarter_used, j * 24 + 4 * (DENSE_UNITS + c) + 4)
                dve.wait_ge(a_turned[b], j * 4 + c + 1)
                dve.tensor_scalar(glu[:, b, :], hid[:, :, 0], LIMIT, None, ALU.min).then_inc(glu_set, 1)
                dve.tensor_scalar(lin[:, b, :], hid[:, :, 1], LIMIT, 1.0, ALU.min, ALU.add).then_inc(hid_taken, 1)

            def aT(j, c, b):
                dve.wait_ge(aT_hi, j * 8 + 2 * c + b + 1)
                dve.tensor_tensor(aTl[:, 2 * c:2 * c + 2, b, :], ps[:, 4 + b, 0:256].rearrange("p (k n) -> p k n", k=2),
                                  aTh[:, 2 * c:2 * c + 2, b, :].bitcast(F32), ALU.subtract).then_inc(aT_lo, 1)

            for q in range(3):
                jsplit(0, 0, q)
            for r in range(4):
                xT(0, r)
            dve.sem_inc(aT_lo, 2)
            with dve.Fori(0, JOBS, 1) as j:
                left = dve.value_load(jobt[0:1, 2, bass.ds(j, 1)], min_val=0, max_val=T)
                with dve.If(left > 0):
                    for c in range(JOB_UNITS):
                        if 2 <= c <= 3:
                            aT(j, c - 2, 0)
                            aT(j, c - 2, 1)
                        jsplit(j, c + 1, 0)
                        jsplit(j, c + 1, 1)
                        if 1 <= c <= 3:
                            hidden(j, c - 1, 0)
                        jsplit(j, c + 1, 2)
                        if 1 <= c <= 3:
                            hidden(j, c - 1, 1)
                        if c == 3:
                            hidden(j, 3, 0)
                            hidden(j, 3, 1)
                            aT(j, 2, 0)
                            aT(j, 2, 1)
                            for r in range(4):
                                xT(j + 1, r)
                            aT(j, 3, 0)
                            aT(j, 3, 1)

            dve.wait_ge(gfin_in, 16)
            for t in range(NT):
                invert(rstd[:, t:t + 1], 2 * NT + 2 + t + 1)
                dve.scalar_tensor_tensor(out=mix[:, t, :], in0=mix[:, t, :], scalar=rstd[:, t:t + 1],
                                         in1=g2row[:, :], op0=ALU.mult, op1=ALU.mult).then_inc(fset, 1)

        @block.gpsimd
        def _(pool):
            steps = [0]

            def link(ins):
                steps[0] += 1
                ins.then_inc(pool_step, 1)
                pool.wait_ge(pool_step, steps[0])

            def select(o, pattern, cm, base_, fill=0.0, op=ALU.is_ge):
                link(pool.affine_select(out=o, in_=o, compare_op=op, fill=fill, base=base_,
                                        pattern=pattern, channel_multiplier=cm))

            def iota(o, pattern, cm, base_=0):
                link(pool.iota(o, pattern=pattern, base=base_, channel_multiplier=cm,
                               allow_small_or_imprecise_dtypes=True))

            def split(n, q):
                cols = 256 if n == 3 else UNIT
                pool.wait_ge(split_hi, 4 * n + q + 1)
                pool.tensor_tensor(wlo[:, q, :, 0:cols], raw[:, q, :, 0:cols], whi[:, q, :, 0:cols].bitcast(F32),
                                   ALU.subtract).then_inc(split_lo_pool, 1)

            pool.memset(epsc[:, :], EPS).then_inc(eps_set, 1)
            link(pool.memset(ident[:, :], 0.0))
            select(ident[:, :], [[-1, P]], 1, 0, 1.0, ALU.not_equal)
            link(pool.memset(ones2[:, :].bitcast(F32), 1.0))
            pool.sem_inc(const_set, 1)
            link(pool.memset(tinit[:, :, :], 0.0))
            iota(tinit[:, :, 0], [[1, JOB_T]], 0, T)
            pool.dma_start(table_d.rearrange("(p n) w -> p n w", p=P), tinit[:, :, :]).then_inc(tinit_out, 16)
            split(0, 3)
            iota(dist[:, :], [[-1, 2 * P]], 1, P)
            link(pool.memset(closed[:, :], 0.0))
            select(closed[:, :], [[-1, 2 * P]], 1, P, NEG)
            select(closed[:, :], [[1, 2 * P]], -1, -1, NEG)
            link(pool.memset(maskL[:, :, :], 1))
            for L in range(LEVELS):
                h = 64 >> L
                m = maskL[:, L, :].rearrange("p (m h) -> p m h", h=h)
                select(m, [[-2 * h, 64 // h], [0, h]], 1, 0)
                select(m, [[2 * h, 64 // h], [0, h]], -1, h - 1)
            link(pool.memset(onesf[:, :], 1.0))
            link(pool.memset(before[:, :], 1.0))
            select(before[:, :], [[1, P]], -1, -1)
            pool.sem_inc(const_set, 1)
            pool.wait_ge(bias_hi, 1)
            pool.tensor_tensor(bpl[:, :], bp[:, :], bph[:, :].bitcast(F32), ALU.subtract).then_inc(bias_lo, 1)
            for n in range(6):
                if n == 5:
                    for c in range(8):
                        pool.wait_ge(*taken(5, c))
                        pool.dma_start(hg_d[c * P:(c + 1) * P, :], hgs[:, c % 2, :]).then_inc(hg_out[c % 2], 16)
                split(n + 1, 3)

            pool.wait_ge(quarter_used, 4 * 6)
            link(pool.memset(reset[:, :], 1.0))
            link(pool.memset(reset[:, :].rearrange("p (t n) -> p t n", n=P)[:, :, 0:1], 0.0))
            pool.sem_inc(reset_set, 1)
            pool.wait_ge(keys_set, HH)
            for s in range(STEPS * HH):
                hd, L = divmod(s, STEPS)
                pool.wait_ge(exp_set, s + 1)
                if s >= 2:
                    pool.wait_ge(level_used, s - 1)
                if L < LEVELS:
                    h = 64 >> L
                    o, k, e = (z.rearrange("p (m two h) -> p m two h", two=2, h=h)[:, :, 0, :]
                               for z in (hp[:, s % 2, :], hk[:, hd, :], he[:, s % 2, :]))
                    pool.tensor_tensor(o, k, e, ALU.mult).then_inc(prod_pool, 1)
                elif L == LEVELS:
                    pool.tensor_tensor(hp[:, s % 2, :], hk[:, hd, :], he[:, s % 2, :], ALU.mult).then_inc(prod_pool, 1)

            pool.wait_ge(hgt_in, 16)
            pool.wait_ge(gmix_in, 32)
            pool.tensor_tensor(hgt[:, :, :], hgt[:, :, :],
                               grow[:, 512:].unsqueeze(1).broadcast_to([P, NT, 512]), ALU.mult).then_inc(hgt_set, 1)
            pool.wait_ge(msq, 5 * NT)
            link(pool.memset(zero[:, :], 0.0))
            pool.sem_inc(zero_set, 1)
            iota(iotaE[:, :], [[1, NE]], 0)
            iota(tok[:, :], [[P, NT]], 1)
            iota(jobi[:, :], [[1, JT_W]], 0)
            iota(eid[:, :], [[0, 1]], 1)
            pool.wait_ge(late_in, 48)
            pool.sem_inc(late_set, 1)
            split(7, 3)
            for t in range(NT):
                pool.wait_ge(pos_set, t + 1)
                for k in range(TOPK):
                    pool.indirect_dma_start(out=table_d, out_offset=bass.IndirectOffsetOnAxis(ap=pos[:, t, k:k + 1], axis=0),
                                            in_=load[:, t, k, :], in_offset=None).then_inc(table_out, 16)
            pool.wait_ge(jobs_set, 1)
            pool.wait_ge(table_out, 16 * NT * TOPK)
            tview = table_d.rearrange("(m p) w -> p m w", p=P)

            def wait(semaphore, value):
                pool.wait_ge(semaphore, value)
                pool.sem_inc(pool_mark, 1)

            def load_slots(j):
                part = pool.value_load(jobt[0:1, 1, bass.ds(j, 1)], min_val=0, max_val=NE * 4 - 1)
                pool.dma_start(tnext[:, :, :], tview[:, bass.ds(part * 2, 2), :]).then_inc(tnext_in, 16)

            def gather(j):
                wait(tnext_in, j * 16 + 16)
                pool.tensor_copy(inext[:, :], tnext[:, :, 0]).then_inc(tnext_cast, 1)
                wait(tnext_cast, j + 1)
                for b in range(2):
                    pool.indirect_dma_start(out=xg[:, b, :], out_offset=None, in_=h2_d,
                                            in_offset=bass.IndirectOffsetOnAxis(ap=inext[:, b:b + 1], axis=0)
                                            ).then_inc(gathered, 16)

            def jsplit(j, c):
                wait(split_hi, j * 24 + 4 * (DENSE_UNITS + c) + 4)
                pool.tensor_tensor(wlo[:, 3, :, :], raw[:, 3, :, :], whi[:, 3, :, :].bitcast(F32),
                                   ALU.subtract).then_inc(split_lo_pool, 1)

            def activate(j, c, b):
                wait(hid_taken, j * 8 + 2 * c + b + 1)
                pool.tensor_scalar(lin[:, b, :], lin[:, b, :], 1.0 - LIMIT, None, ALU.max)
                wait(sig_set, j * 8 + 2 * c + b + 1)
                pool.tensor_tensor(sig[:, b, :], sig[:, b, :], glu[:, b, :], ALU.mult).then_inc(swish_set, 1)
                wait(swish_set, j * 8 + 2 * c + b + 1)
                pool.tensor_tensor(glu[:, b, :], lin[:, b, :], sig[:, b, :], ALU.mult).then_inc(act_set, 1)

            pool.wait_ge(h2_out[0], 64)
            pool.wait_ge(h2_out[1], 64)
            pool.wait_ge(acc_out, 128)
            pool.wait_ge(pads_out, 64)
            load_slots(0)
            gather(0)
            jsplit(0, 0)
            with pool.Fori(0, JOBS, 1) as j:
                left = pool.value_load(jobt[0:1, 2, bass.ds(j, 1)], min_val=0, max_val=T)
                with pool.If(left > 0):
                    pool.tensor_copy(icur[:, :], tnext[:, :, 0])
                    pool.tensor_copy(gcur[:, :], tnext[:, :, 1]).then_inc(tcur_set, 1)
                    wait(tcur_set, j + 1)
                    load_slots(j + 1)
                    for c in range(JOB_UNITS):
                        if c == 1:
                            wait(x_turned, j * 4 + 4)
                            gather(j + 1)
                        if 1 <= c <= 3:
                            activate(j, c - 1, 0)
                            activate(j, c - 1, 1)
                        jsplit(j, c + 1)
                        if c == 3:
                            activate(j, 3, 0)
                            activate(j, 3, 1)
                    wait(y_set, j * 4 + 8)
                    for b in range(2):
                        pool.indirect_dma_start(out=acc_d, out_offset=bass.IndirectOffsetOnAxis(ap=icur[:, b:b + 1], axis=0),
                                                in_=y[:, b, :], in_offset=None, compute_op=ALU.add).then_inc(scattered, 16)
                    wait(scattered, j * 32 + 32)
            pool.sem_inc(jobs_over, 1)


_INS = ["x", "norm1_g", "w_in", "b_in", "attn_sinks", "attn_out_g", "hgrn_lb_logits", "hgrn_out_g",
        "w_out", "b_out", "norm2_g", "router_w", "router_b", "w1", "b1", "w2", "b2", "final_g"]


def kernel(**inputs):
    import numpy as np
    import concourse.bacc as bacc
    from concourse import mybir
    from concourse.bass_utils import run_bass_kernel_spmd

    nc = bacc.Bacc("TRN2", target_bir_lowering=False, num_devices=1)
    arrays, args = {}, []
    for name in _INS:
        a = np.ascontiguousarray(inputs[name])
        arrays[f"in_{name}"] = a
        args.append(nc.dram_tensor(f"in_{name}", a.shape, mybir.dt.from_np(a.dtype), kind="ExternalInput").ap())
    args.append(nc.dram_tensor("out_0", (1, T, D), mybir.dt.from_np(np.dtype("float32")), kind="ExternalOutput").ap())
    build(nc, *args)
    r = run_bass_kernel_spmd(nc, [arrays], core_ids=[0])
    return r.results[0]["out_0"]
```

```python
from contextlib import ExitStack

import concourse.bass as bass
from concourse import mybir

P = 128
D = 1024
T = 1024
NT = T // P
KT = D // P
QUARTERS = 4
UNIT = 512
NQ, NKV, HD = 8, 2, 64
GROUP = NQ // NKV
HH = 4
ATTN_W = NQ * HD
C_AQ = 0
C_AK = ATTN_W
C_AV = C_AK + NKV * HD
C_HQ = C_AV + NKV * HD
C_HF = C_HQ + HH * P
C_HI = C_HF + HH * P
C_HG = C_HI + HH * P
NE = 32
TOPK = 4
FF = 1024
JOB_T = 256
JOBS = T * TOPK // JOB_T + NE - 1
JT_W = JOBS + 1
PAD_ROWS = JOB_T
EPS = 1e-5
NEG = -1e30
LIMIT = 7.0
ALPHA = 1.702
DENSE_UNITS = 8
JOB_UNITS = 6
LEVELS = 7
STEPS = LEVELS + 2
BW = 2 * FF + D
B_AV, B_HI, B_HG, B_OUT = 0, 128, 640, 1152

F32 = mybir.dt.float32
F32R = mybir.dt.float32r
I32 = mybir.dt.int32
U32 = mybir.dt.uint32
ALU = mybir.AluOpType
ACT = mybir.ActivationFunctionType
AX = mybir.AxisListType.X
SLOPES = [2.0 ** (-8.0 * (h + 1) / NQ) for h in range(NQ)]


def build(nc, x, norm1_g, w_in, b_in, attn_sinks, attn_out_g, hgrn_lb_logits, hgrn_out_g, w_out,
          b_out, norm2_g, router_w, router_b, w1, b1, w2, b2, final_g, out):
    x, out = x[0], out[0]
    w_in, w_out, w1, w2 = w_in[0], w_out[0], w1[0], w2[0]
    KB = 1024
    base = (nc.sbuf_base + 31) // 32 * 32

    def at(name, offset, shape, dt=F32):
        return nc.alloc_sbuf_tensor_at(name, shape, dt, offset=base + int(offset))

    def dram(name, shape, dt=F32):
        return nc.dram_tensor(name, shape, dt, kind="Internal").ap()

    h2_d = dram("h2_d", (T + PAD_ROWS, D))
    acc_d = dram("acc_d", (T + PAD_ROWS, D))
    table_d = dram("table_d", (NE * T, 2))
    hg_d = dram("hg_d", (T, 512))
    brow_d = dram("brow_d", (NE + 1, 2, BW))

    raw = at("raw", 0, [P, QUARTERS, 2, UNIT])
    whi = at("whi", 16 * KB, [P, QUARTERS, 2, UNIT], F32R)
    wlo = at("wlo", 32 * KB, [P, QUARTERS, 2, UNIT], F32R)
    A = 48 * KB
    th = at("th", A, [P, KT, T], F32R)
    tl = at("tl", A + 32 * KB, [P, KT, T], F32R)
    mix = at("mix", A, [P, NT, D])
    alibi = at("alibi", A + 32 * KB, [P, NQ, 2 * P])
    score = at("score", A + 40 * KB, [P, 2, GROUP, 2 * P])
    probT = at("probT", A + 48 * KB, [P, 2, GROUP, P])
    hk = at("hk", A + 32 * KB, [P, HH, T])
    reset = at("reset", A + 52 * KB, [P, T])
    attT = [at("attT0", A + 48 * KB, [P, NT, P]), at("attT1", A + 56 * KB, [P, NT, P])]
    stat = at("stat", A + 60 * KB, [P, 6, 2 * NT, GROUP])
    hgt = at("hgt", A + 32 * KB, [P, NT, 512])
    junk = at("junk", A + 48 * KB, [P, D])
    h2 = at("h2", A + 32 * KB, [P, 2, D])
    h2Th = at("h2Th", A + 40 * KB, [P, KT, P], F32R)
    h2Tl = at("h2Tl", A + 44 * KB, [P, KT, P], F32R)
    g2row = at("g2row", A + 52 * KB, [P, D])
    zero = at("zero", A + 56 * KB, [P, D])
    raw2 = at("raw2", A, [P, QUARTERS, 2, UNIT])
    whi2 = at("whi2", A + 16 * KB, [P, QUARTERS, 2, UNIT], F32R)
    wlo2 = at("wlo2", A + 32 * KB, [P, QUARTERS, 2, UNIT], F32R)
    raws, whis, wlos = (raw, raw2), (whi, whi2), (wlo, wlo2)
    B = 112 * KB
    xs = at("xs", B, [P, NT, D])
    bp = at("bp", B + 32 * KB, [NE + 1, BW])
    bph = at("bph", B + 44 * KB, [NE + 1, BW], F32R)
    bpl = at("bpl", B + 56 * KB, [NE + 1, BW], F32R)
    tinit = at("tinit", B + 68 * KB, [P, JOB_T, 2])
    hf = at("hf", B, [P, HH, T])
    hq = at("hq", B + 16 * KB, [P, HH, T])
    hv = at("hv", B + 32 * KB, [P, NT, 512])
    aq = at("aq", B + 48 * KB, [P, GROUP, T])
    ak = at("ak", B + 64 * KB, [P, P + T])
    av = at("av", B + 68.5 * KB, [P, NT, P])
    he = at("he", B + 48 * KB, [P, 2, T])
    hp = at("hp", B + 56 * KB, [P, 2, T])
    kbT = at("kbT", B + 64 * KB, [P, NT, P])
    state = at("state", B + 68 * KB, [P, NT, P])
    mh = at("mh", B, [P, KT, T], F32R)
    ml = at("ml", B + 32 * KB, [P, KT, T], F32R)
    xTh = at("xTh", B, [P, KT, 2, P], F32R)
    xTl = at("xTl", B + 8 * KB, [P, KT, 2, P], F32R)
    aTh = at("aTh", B + 16 * KB, [P, KT, 2, P], F32R)
    aTl = at("aTl", B + 24 * KB, [P, KT, 2, P], F32R)
    xg = at("xg", B + 32 * KB, [P, 2, D])
    y = at("y", B + 40 * KB, [P, 2, D])
    glu = at("glu", B + 48 * KB, [P, 2, 256])
    lin = at("lin", B + 50 * KB, [P, 2, 256])
    sig = at("sig", B + 52 * KB, [P, 2, 256])
    R = [B + 72.5 * KB]

    def rest(name, shape, dt=F32):
        words = 1
        for n in shape[1:]:
            words *= n
        tensor = at(name, R[0], shape, dt)
        R[0] += (words * 4 + 31) // 32 * 32
        return tensor

    junk0 = at("junk0", R[0], [P, D])
    brow = rest("brow", [2, BW], F32R)
    grow = rest("grow", [P, D])
    hgs = at("hgs", R[0] - 4 * KB, [P, 2, 512])
    ident = rest("ident", [P, P])
    epsc = rest("epsc", [P, 1])
    ones2 = rest("ones2", [2, P], F32R)
    dist = rest("dist", [P, 2 * P])
    closed = rest("closed", [P, 2 * P])
    maskL = rest("maskL", [P, LEVELS, 64], I32)
    before = at("before", R[0], [P, P])
    onesf = at("onesf", R[0] + 512, [P, P])
    R[0] += 1024
    bcol = rest("bcol", [P, 13])
    sinks = rest("sinks", [P, NQ])
    lbl = rest("lbl", [P, 2, HH])
    lbe = rest("lbe", [P, 2, HH])
    lbm = rest("lbm", [P, HH])
    lb = rest("lb", [P, HH])
    oml = rest("oml", [P, HH])
    ss = rest("ss", [P, NT])
    rstd = rest("rstd", [P, NT])
    decay = rest("decay", [P, NT])
    ssa = rest("ssa", [P, NT, 5])
    rsa = rest("rsa", [P, NT, 5])
    assert base + R[0] <= nc.sbuf_usable_end, R[0] / KB
    Z = [A + 60 * KB]

    def late(name, shape, dt=F32):
        words = 1
        for n in shape[1:]:
            words *= n
        tensor = at(name, Z[0], shape, dt)
        Z[0] += (words * 4 + 31) // 32 * 32
        assert Z[0] <= A + 64 * KB
        return tensor

    rb = late("rb", [P, NE])
    iotaE = late("iotaE", [P, NE])
    logit = late("logit", [P, NE])
    top = late("top", [P, 8])
    topi = late("topi", [P, 8], U32)
    topf = late("topf", [P, 8])
    ntop = late("ntop", [P, 1])
    gexp = late("gexp", [P, TOPK])
    gden = late("gden", [P, 1])
    grec = late("grec", [P, 1])
    hot = late("hot", [P, TOPK, NE])
    count = late("count", [P, NT + 1, NE])
    picked = late("picked", [P, NE])
    rank = late("rank", [P, TOPK])
    posf = late("posf", [P, TOPK])
    tok = late("tok", [P, NT])
    B2 = B + 66 * KB
    rw = at("rw", B2, [P, KT, NE])
    rwh = at("rwh", B2 + KB, [P, KT, NE], F32R)
    rwl = at("rwl", B2 + 2 * KB, [P, KT, NE], F32R)
    pos = at("pos", B2 + 3 * KB, [P, NT, TOPK], I32)
    load = at("load", B2 + 3.25 * KB, [P, NT, TOPK, 2])
    nexp = at("nexp", B2 + 3.5 * KB, [NE, 4])
    eid = at("eid", B2 + 3.53125 * KB, [NE, 1])
    jobi = at("jobi", B2 + 3.5625 * KB, [NE, JT_W])
    jobm = at("jobm", B2 + 3.75 * KB, [NE, 2, JT_W])
    jobr = at("jobr", B2 + 4.25 * KB, [NE, 3, JT_W])
    jobt = at("jobt", B2 + 5 * KB, [1, 3, JT_W], I32)
    tnext = at("tnext", B2 + 5.75 * KB, [P, 2, 2])
    inext = at("inext", B2 + 5.78125 * KB, [P, 2], I32)
    icur = at("icur", B2 + 5.8125 * KB, [P, 2], I32)
    gcur = at("gcur", B2 + 5.84375 * KB, [P, 2])

    ctx = ExitStack()
    with ctx:
        ps = ctx.enter_context(nc.psum_tensor("ps", [P, 8, 512], F32))

        def sem(name):
            return ctx.enter_context(nc.semaphore(name))

        x_in = [sem(f"x_in{t}") for t in range(NT)]
        const_in, bias_in, bias_hi, bias_lo, bias_out, brow_in = (
            sem(n) for n in ("const_in", "bias_in", "bias_hi", "bias_lo", "bias_out", "brow_in"))
        bp_zero, tinit_out, const_set, pool_step, dve_step = (
            sem(n) for n in ("bp_zero", "tinit_out", "const_set", "pool_step", "dve_step"))
        lb_max, lb_exp = sem("lb_max"), sem("lb_exp")
        squared, normed, turned, turned_hi, turned_lo = (
            sem(n) for n in ("squared", "normed", "turned", "turned_hi", "turned_lo"))
        raw_in = [sem(f"raw_in{q}") for q in range(QUARTERS)]
        raw2_in = [sem(f"raw2_in{q}") for q in range(QUARTERS)]
        split_hi, split_lo_dve, split_lo_pool, quarter_used = (
            sem(n) for n in ("split_hi", "split_lo_dve", "split_lo_pool", "quarter_used"))
        chain_done, taken_act, taken_dve = sem("chain_done"), sem("taken_act"), sem("taken_dve")
        hg_out = [sem("hg_out0"), sem("hg_out1")]
        scored, score_added, maxed, exped, sinked, probs_turned, pT_act, pT_dve, heads_done, heads_out = (
            sem(n) for n in ("scored", "score_added", "maxed", "exped", "sinked", "probs_turned",
                             "pT_act", "pT_dve", "heads_done", "heads_out"))
        reset_set, keys_set, logs_set, sums_set = (
            sem(n) for n in ("reset_set", "keys_set", "logs_set", "sums_set"))
        arg_set, exp_set, prod_dve, prod_pool, diag_done, level_used, level_copied = (
            sem(n) for n in ("arg_set", "exp_set", "prod_dve", "prod_pool", "diag_done",
                             "level_used", "level_copied"))
        kbT_set, added_state, states_set, rec_out = (
            sem(n) for n in ("kbT_set", "added_state", "states_set", "rec_out"))
        gmix_in, hgt_in, hgt_set, msq, mnormed, mturned, mturned_hi, mturned_lo = (
            sem(n) for n in ("gmix_in", "hgt_in", "hgt_set", "msq", "mnormed", "mturned",
                             "mturned_hi", "mturned_lo"))
        xr_in, late_in, late_set, x2_set, sq2, h2_set, h2_turned, h2_hi, h2_lo = (
            sem(n) for n in ("xr_in", "late_in", "late_set", "x2_set", "sq2", "h2_set",
                             "h2_turned", "h2_hi", "h2_lo"))
        h2_out = [sem("h2_out0"), sem("h2_out1")]
        acc_out, pads_out, zero_set, logits_done, top_set, gate_exp, picked_set, ranked, pos_set = (
            sem(n) for n in ("acc_out", "pads_out", "zero_set", "logits_done", "top_set",
                             "gate_exp", "picked_set", "ranked", "pos_set"))
        rw_hi, rw_lo, table_out = sem("rw_hi"), sem("rw_lo"), sem("table_out")
        jn, jn_set, jbase, jrows, jsum, jobs_set = (
            sem(n) for n in ("jn", "jn_set", "jbase", "jrows", "jsum", "jobs_set"))
        tnext_in, tnext_cast, gathered, tcur_set = (
            sem(n) for n in ("tnext_in", "tnext_cast", "gathered", "tcur_set"))
        brow1_in, brow2_in = sem("brow1_in"), sem("brow2_in")
        x_turned, xT_hi, xT_lo, y_zero, scattered, jobs_over = (
            sem(n) for n in ("x_turned", "xT_hi", "xT_lo", "y_zero", "scattered", "jobs_over"))
        hid_taken, glu_set, prod_set, sig_set, act_set, a_turned, aT_hi, aT_lo, y_set = (
            [sem(f"{n}{b}") for b in range(2)]
            for n in ("hid_taken", "glu_set", "prod_set", "sig_set", "act_set", "a_turned", "aT_hi",
                      "aT_lo", "y_set"))
        rooted, eps_set = sem("rooted"), sem("eps_set")
        pool_mark, sync_mark, act_mark = sem("pool_mark"), sem("sync_mark"), sem("act_mark")
        fin_in = [sem(f"fin_in{t}") for t in range(NT)]
        gfin_in, fsq, fset, fin_out = sem("gfin_in"), sem("fsq"), sem("fset"), sem("fin_out")

        CHAINS = [8, 8, 8, 4, 8, 8, 8, 8]
        BEFORE = [sum(CHAINS[:n]) for n in range(DENSE_UNITS + 1)]

        BY_ACT = [8, 8, 0, 2, 8, 8, 0, 0]
        BY_DVE = [0, 8, 8, 2, 0, 8, 8, 8]

        def taken(n, c):
            if n in (0, 4) or (n == 3 and c >= 2):
                return taken_act, sum(BY_ACT[:n]) + c + 1 - (2 if n == 3 else 0)
            return taken_dve, sum(BY_DVE[:n]) + c + 1

        def args_by(s):
            return (LEVELS + 1) * (s // STEPS) + min(s % STEPS, LEVELS) + 1

        def dve_prods_by(s):
            return (LEVELS + 1) * (s // STEPS) + (s % STEPS) + (s % STEPS < LEVELS)

        def pool_prods_by(s):
            return (LEVELS + 1) * (s // STEPS) + min(s % STEPS, LEVELS) + 1

        def chain_ready(engine, n, c):
            if c < CHAINS[n] - 1:
                engine.wait_ge(chain_done, BEFORE[n] - n + c + 1)
            else:
                engine.wait_ge(quarter_used, 4 * n + 4)

        N_CONST = 2 + 5 + 1 + 1
        U_COLS = [C_HF, C_HQ, C_AQ, C_AK, C_HI, C_HG, 0, UNIT]
        wiv = w_in.rearrange("(q a p) n -> q p a n", q=QUARTERS, p=P)
        wov = w_out.rearrange("(q a p) n -> q p a n", q=QUARTERS, p=P)
        w1v = w1.rearrange("e (q a p) n -> q e p a n", q=QUARTERS, p=P)
        w2v = w2.rearrange("e (q a p) n -> q e p a n", q=QUARTERS, p=P)
        
        def expert_part(view, q, e, cols):
            return view[q, bass.ds(e, 1), :, :, cols].rearrange("o p a n -> (o p) a n")

        def bias_part(e, cols):
            return brow_d[bass.ds(e, 1), :, cols].rearrange("o s n -> (o s) n")

        bview = b_in[0]

        block = ctx.enter_context(nc.Block())

        @block.sync
        def _(sp):
            sp.dma_start(xs[:, 0, :], x[0:P, :]).then_inc(x_in[0], 16)
            sp.dma_start(grow[:, :], norm1_g.broadcast_to([P, D])).then_inc(const_in, 16)
            sp.dma_start(sinks[:, :], attn_sinks.broadcast_to([P, NQ])).then_inc(const_in, 16)
            for t in range(1, 3):
                sp.dma_start(xs[:, t, :], x[t * P:(t + 1) * P, :]).then_inc(x_in[t], 16)

            def weights(n, q):
                cols = 256 if n == 3 else UNIT
                src = wiv if n < 6 else wov
                if n == 2:
                    for a in range(2):
                        for g in range(NKV):
                            sp.dma_start(raw[:, q, a, :].rearrange("p (i g d) -> p g i d", g=NKV, i=GROUP)[:, g],
                                         wiv[q, :, a, 256 * g:256 * g + 256].rearrange("p (i d) -> p i d", i=GROUP)
                                         ).then_inc(raw_in[q], 16)
                    return
                sp.dma_start(raw[:, q, :, 0:cols],
                             src[q, :, :, U_COLS[n]:U_COLS[n] + cols]).then_inc(raw_in[q], 16)

            def raw_free(g, q):
                sp.wait_ge(split_hi, 4 * g + q - 3)
                if q < 3:
                    sp.wait_ge(split_lo_dve, 3 * g + q - 2)
                else:
                    sp.wait_ge(split_lo_pool, g)

            for g in range(NKV):
                sp.dma_start(bcol[64 * g:64 * g + 64, 0:4],
                             bview[g * 256:g * 256 + 256].rearrange("(i p) -> p i", p=64),
                             allow_slow_non_contiguous=True).then_inc(const_in, 16)
            sp.dma_start(bcol[:, 4:5], bview[C_AK:C_AK + P].rearrange("(i p) -> p i", p=P),
                         allow_slow_non_contiguous=True).then_inc(const_in, 16)
            sp.dma_start(bcol[:, 5:9], bview[C_HQ:C_HQ + 512].rearrange("(i p) -> p i", p=P),
                         allow_slow_non_contiguous=True).then_inc(const_in, 16)
            sp.dma_start(bcol[:, 9:13], bview[C_HF:C_HF + 512].rearrange("(i p) -> p i", p=P),
                         allow_slow_non_contiguous=True).then_inc(const_in, 16)
            sp.dma_start(lbl[:, 0, :], hgrn_lb_logits[0].rearrange("(h p) -> p h", p=P),
                         allow_slow_non_contiguous=True).then_inc(const_in, 16)
            sp.dma_start(lbl[:, 1, :], hgrn_lb_logits[1].rearrange("(h p) -> p h", p=P),
                         allow_slow_non_contiguous=True).then_inc(const_in, 16)
            for q in range(QUARTERS):
                weights(0, q)
            for t in range(3, NT):
                sp.dma_start(xs[:, t, :], x[t * P:(t + 1) * P, :]).then_inc(x_in[t], 16)
            sp.wait_ge(bp_zero, 1)
            sp.dma_start(bp[0:NE, 0:2 * FF], b1[0]).then_inc(bias_in, 16)
            sp.dma_start(bp[0:NE, 2 * FF:BW], b2[0]).then_inc(bias_in, 16)
            sp.dma_start(bp[NE:NE + 1, 0:128], b_in[:, C_AV:C_HQ]).then_inc(bias_in, 16)
            sp.dma_start(bp[NE:NE + 1, 128:1152], b_in[:, C_HI:C_HI + D]).then_inc(bias_in, 16)
            sp.dma_start(bp[NE:NE + 1, 1152:2176], b_out).then_inc(bias_in, 16)
            for q in range(QUARTERS):
                raw_free(1, q)
                weights(1, q)
            sp.wait_ge(bias_hi, 1)
            sp.dma_start(brow_d[:, 0, :], bph[:, :].bitcast(F32)).then_inc(bias_out, 16)
            sp.wait_ge(bias_lo, 1)
            sp.dma_start(brow_d[:, 1, :], bpl[:, :].bitcast(F32)).then_inc(bias_out, 16)
            sp.wait_ge(bias_out, 32)
            sp.dma_start(brow[:, :].bitcast(F32), brow_d[NE]).then_inc(brow_in, 16)
            for n in range(2, 7):
                for q in range(QUARTERS):
                    raw_free(n, q)
                    weights(n, q)
            sp.wait_ge(hg_out[0], 16 * 4)
            sp.wait_ge(hg_out[1], 16 * 4)
            sp.dma_start(grow[:, 0:512], attn_out_g.broadcast_to([P, 512])).then_inc(gmix_in, 16)
            sp.dma_start(grow[:, 512:D], hgrn_out_g.broadcast_to([P, 512])).then_inc(gmix_in, 16)
            sp.wait_ge(level_used, STEPS * HH)
            sp.wait_ge(prod_pool, pool_prods_by(STEPS * HH - 1))
            sp.wait_ge(rec_out, 2 * HH)
            sp.dma_start(hgt[:, :, :], hg_d.rearrange("(t p) n -> p t n", p=P)).then_inc(hgt_in, 16)
            sp.dma_start(g2row[:, :], norm2_g.broadcast_to([P, D])).then_inc(late_in, 16)
            sp.dma_start(rb[:, :], router_b.broadcast_to([P, NE])).then_inc(late_in, 16)
            sp.wait_ge(mturned, 2 * NT)
            sp.dma_start(mix[:, :, :], x.rearrange("(t p) n -> p t n", p=P)).then_inc(xr_in, 16)
            sp.dma_start(rw[:, :, :], router_w[0].rearrange("(k p) e -> p k e", p=P)).then_inc(late_in, 16)
            for q in range(QUARTERS):
                raw_free(7, q)
                weights(7, q)
            sp.wait_ge(zero_set, 1)
            for i in range(PAD_ROWS // P):
                sp.dma_start(h2_d[T + i * P:T + (i + 1) * P, :], zero[:, :]).then_inc(pads_out, 16)
                sp.dma_start(acc_d[T + i * P:T + (i + 1) * P, :], zero[:, :]).then_inc(pads_out, 16)
            for t in range(NT):
                sp.wait_ge(x2_set, t + 1)
                sp.dma_start(acc_d[t * P:(t + 1) * P, :], mix[:, t, :]).then_inc(acc_out, 16)
                sp.wait_ge(h2_set, t + 1)
                sp.dma_start(h2_d[t * P:(t + 1) * P, :], h2[:, t % 2, :]).then_inc(h2_out[t % 2], 16)

            def wait(semaphore, value):
                sp.wait_ge(semaphore, value)
                sp.sem_inc(sync_mark, 1)

            sp.wait_ge(jobs_set, 1)
            e0 = sp.value_load(jobt[0:1, 0, 0:1], min_val=0, max_val=NE - 1)
            for q in range(QUARTERS):
                raw_free(DENSE_UNITS, q)
                sp.dma_start(raw[:, q, :, :], expert_part(w1v, q, e0, slice(0, UNIT))).then_inc(raw_in[q], 16)
            sp.wait_ge(acc_out, 16 * NT)
            for q in range(QUARTERS):
                sp.dma_start(raw2[:, q, :, :], expert_part(w1v, q, e0, slice(UNIT, 2 * UNIT))).then_inc(raw2_in[q], 16)
            with sp.Fori(0, JOBS, 1) as j:
                left = sp.value_load(jobt[0:1, 2, bass.ds(j, 1)], min_val=0, max_val=T)
                with sp.If(left > 0):
                    e = sp.value_load(jobt[0:1, 0, bass.ds(j, 1)], min_val=0, max_val=NE - 1)
                    en = sp.value_load(jobt[0:1, 0, bass.ds(j + 1, 1)], min_val=0, max_val=NE - 1)
                    for c in range(2, JOB_UNITS + 2):
                        for q in range(QUARTERS):
                            wait(split_hi, j * 24 + 4 * (DENSE_UNITS + c) + q - 7)
                            if q < 3:
                                wait(split_lo_dve, j * 18 + 3 * (DENSE_UNITS + c) + q - 5)
                            else:
                                wait(split_lo_pool, j * 6 + DENSE_UNITS + c - 1)
                            if c < 4:
                                src = expert_part(w1v, q, e, slice(c * UNIT, (c + 1) * UNIT))
                            elif c < 6:
                                src = expert_part(w2v, q, e, slice((c - 4) * UNIT, (c - 3) * UNIT))
                            else:
                                src = expert_part(w1v, q, en, slice((c - 6) * UNIT, (c - 5) * UNIT))
                            sp.dma_start(raws[c % 2][:, q, :, :], src).then_inc((raw_in, raw2_in)[c % 2][q], 16)
            sp.dma_start(g2row[:, :], final_g.rearrange("(a d) -> a d", a=1).broadcast_to([P, D])).then_inc(gfin_in, 16)
            sp.wait_ge(jobs_over, 3)
            for t in range(NT):
                sp.dma_start(mix[:, t, :], acc_d[t * P:(t + 1) * P, :]).then_inc(fin_in[t], 16)
            for t in range(NT):
                sp.wait_ge(fset, t + 1)
                sp.dma_start(out[t * P:(t + 1) * P, :], mix[:, t, :]).then_inc(fin_out, 16)
            sp.wait_ge(fin_out, 16 * NT)

        @block.tensor
        def _(pe):
            def mm3(o, sh, sl, mh_, ml_, start, stop, skip=False):
                pe.matmul(o, sh, mh_, start=start, stop=False, skip_group_check=skip)
                pe.matmul(o, sh, ml_, start=False, stop=False, skip_group_check=skip)
                return pe.matmul(o, sl, mh_, start=False, stop=stop, skip_group_check=skip)

            pe.wait_ge(const_set, 1)
            for t in range(NT):
                pe.wait_ge(normed, t + 1)
                for half in range(2):
                    i = 2 * t + half
                    if i >= 8:
                        pe.wait_ge(turned_lo, i - 7)
                    for k in range(4):
                        m = pe.transpose(ps[:, i % 8, k * P:(k + 1) * P],
                                         xs[:, t, (4 * half + k) * P:(4 * half + k + 1) * P], ident[:, :])
                    m.then_inc(turned, 1)

            def split_ready(n, q):
                pe.wait_ge(split_hi, 4 * n + q + 1)
                if q < 3:
                    pe.wait_ge(split_lo_dve, 3 * n + q + 1)
                else:
                    pe.wait_ge(split_lo_pool, n + 1)

            def unit(n, sth, stl):
                feature_major = n < 3
                for q in range(QUARTERS):
                    split_ready(n, q)
                    for c in range(CHAINS[n]):
                        if q == 0 and n >= 1 and c < CHAINS[n - 1]:
                            pe.wait_ge(*taken(n - 1, c))
                        if q == 0 and n == 4 and c >= CHAINS[3]:
                            pe.wait_ge(*taken(2, c))
                        first, last = q == 0, q == QUARTERS - 1
                        if feature_major or (n == 3 and c < 2):
                            for a in range(2):
                                k = 2 * q + a
                                f = 0 if n == 3 else c // 2
                                h_, l_ = (w[:, q, a, f * P:(f + 1) * P] for w in (whi, wlo))
                                half = c % 2
                                m = mm3(ps[:, c, :], h_, l_, sth[:, k, half * 512:half * 512 + 512],
                                        stl[:, k, half * 512:half * 512 + 512],
                                        first and a == 0, last and a == 1)
                        elif n == 3:
                            for t in range(4 * (c - 2), 4 * (c - 2) + 4):
                                o = ps[:, c, (t % 4) * P:(t % 4 + 1) * P]
                                if first:
                                    pe.matmul(o, ones2[:, :], brow[:, B_AV:B_AV + P], start=t % 4 == 0,
                                              stop=False, skip_group_check=True)
                                for a in range(2):
                                    k = 2 * q + a
                                    m = mm3(o, sth[:, k, t * P:(t + 1) * P], stl[:, k, t * P:(t + 1) * P],
                                            whi[:, q, a, P:2 * P], wlo[:, q, a, P:2 * P],
                                            False, last and a == 1, True)
                        else:
                            if first:
                                b = {4: B_HI, 5: B_HG, 6: B_OUT, 7: B_OUT + UNIT}[n]
                                pe.matmul(ps[:, c, :], ones2[:, :], brow[:, b:b + UNIT], start=True, stop=False)
                            for a in range(2):
                                k = 2 * q + a
                                m = mm3(ps[:, c, :], sth[:, k, c * P:(c + 1) * P], stl[:, k, c * P:(c + 1) * P],
                                        whi[:, q, a, :], wlo[:, q, a, :], False, last and a == 1)
                        if last and c < CHAINS[n] - 1:
                            m.then_inc(chain_done, 1)
                    m.then_inc(quarter_used, 1)

            pe.wait_ge(turned_lo, 2 * NT)
            for n in range(3):
                unit(n, th, tl)
            pe.wait_ge(brow_in, 16)
            for n in range(3, 6):
                unit(n, th, tl)

            pe.wait_ge(*taken(5, 7))

            def scores(b):
                n, kv = divmod(b, 2)
                if b >= 2:
                    pe.wait_ge(score_added, b - 1)
                lo = P if n == 0 else 0
                for i in range(GROUP):
                    m = pe.matmul(ps[:, 2 * kv + i // 2, (i % 2) * 256 + lo:(i % 2) * 256 + 256],
                                  aq[64 * kv:64 * kv + 64, i, n * P:(n + 1) * P],
                                  ak[64 * kv:64 * kv + 64, n * P + lo:n * P + 256],
                                  start=True, stop=True)
                m.then_inc(scored, 1)

            scores(0)
            for b in range(2 * NT):
                n, kv = divmod(b, 2)
                if b + 1 < 2 * NT:
                    scores(b + 1)
                pe.wait_ge(exped, b + 1)
                if b >= 1:
                    pe.wait_ge(pT_act, b)
                    pe.wait_ge(pT_dve, b)
                for half in range(2):
                    if n == 0 and half == 0:
                        pe.sem_inc(probs_turned, 1)
                        continue
                    for i in range(GROUP):
                        m = pe.transpose(ps[:, 4 + half, i * P:(i + 1) * P],
                                         score[:, kv, i, half * P:half * P + P], ident[:, :])
                    m.then_inc(probs_turned, 1)
                pe.wait_ge(pT_act, b + 1)
                pe.wait_ge(pT_dve, b + 1)
                if b >= 2:
                    pe.wait_ge(heads_out, b - 1)
                for i in range(GROUP):
                    o = ps[:, 6 + kv, i * HD:(i + 1) * HD]
                    if n > 0:
                        pe.matmul(o, probT[:, 0, i, :], av[:, n - 1, kv * HD:kv * HD + HD], start=True, stop=False)
                    m = pe.matmul(o, probT[:, 1, i, :], av[:, n, kv * HD:kv * HD + HD], start=n == 0, stop=True)
                m.then_inc(heads_done, 1)

            pe.wait_ge(heads_out, 2 * NT)
            for hd in range(HH):
                if hd == 0:
                    pe.wait_ge(keys_set, HH)
                else:
                    pe.wait_ge(rec_out, 2 * hd)
                for t in range(NT):
                    m = pe.matmul(ps[:, 2 + t // 4, (t % 4) * P:(t % 4 + 1) * P],
                                  hk[:, hd, t * P:(t + 1) * P], hq[:, hd, t * P:(t + 1) * P],
                                  start=True, stop=True)
                m.then_inc(diag_done, 1)
                for L in range(LEVELS):
                    s = STEPS * hd + L
                    lev = LEVELS * hd + L
                    h = 64 >> L
                    pe.wait_ge(prod_dve, dve_prods_by(s))
                    pe.wait_ge(prod_pool, pool_prods_by(s))
                    if lev >= 2:
                        pe.wait_ge(level_copied, lev - 1)
                    for t in range(NT):
                        v = hp[:, s % 2, t * P:(t + 1) * P]
                        m = pe.matmul(ps[:, lev % 2, t * 64:(t + 1) * 64], v,
                                      v.rearrange("p (m two h) -> p m two h", two=2, h=h)[:, :, 1, :],
                                      start=True, stop=True)
                    m.then_inc(level_used, 1)
                s = STEPS * hd + LEVELS
                pe.wait_ge(prod_pool, pool_prods_by(s))
                if hd > 0:
                    pe.wait_ge(kbT_set, 2 * hd)
                for t in range(NT):
                    m = pe.transpose(ps[:, 4 + t // 4, (t % 4) * P:(t % 4 + 1) * P],
                                     hp[:, s % 2, t * P:(t + 1) * P], ident[:, :])
                m.then_inc(level_used, 1)
                pe.wait_ge(kbT_set, 2 * hd + 2)
                if hd > 0:
                    pe.wait_ge(states_set, hd)
                for t in range(NT - 1):
                    m = pe.matmul(ps[:, 6 + t // 4, (t % 4) * P:(t % 4 + 1) * P], kbT[:, t, :],
                                  hv[:, t, hd * P:(hd + 1) * P], start=True, stop=True)
                m.then_inc(added_state, 1)
                s = STEPS * hd + LEVELS + 1
                pe.wait_ge(prod_dve, dve_prods_by(s))
                pe.wait_ge(level_copied, LEVELS * (hd + 1))
                pe.wait_ge(states_set, hd + 1)
                for t in range(NT):
                    o = ps[:, 2 + t // 4, (t % 4) * P:(t % 4 + 1) * P]
                    m = pe.matmul(o, attT[hd % 2][:, t, :], hv[:, t, hd * P:(hd + 1) * P],
                                  start=True, stop=t == 0)
                    if t > 0:
                        m = pe.matmul(o, hp[:, s % 2, t * P:(t + 1) * P], state[:, t - 1, :],
                                      start=False, stop=True)
                m.then_inc(level_used, 1)

            pe.wait_ge(rec_out, 2 * HH)
            for t in range(NT):
                pe.wait_ge(mnormed, t + 1)
                for half in range(2):
                    i = 2 * t + half
                    if i >= 8:
                        pe.wait_ge(mturned_lo, i - 7)
                    for k in range(4):
                        m = pe.transpose(ps[:, i % 8, k * P:(k + 1) * P],
                                         mix[:, t, (4 * half + k) * P:(4 * half + k + 1) * P], ident[:, :])
                    m.then_inc(mturned, 1)
            pe.wait_ge(mturned_lo, 2 * NT)
            unit(6, mh, ml)
            unit(7, mh, ml)

            pe.wait_ge(*taken(7, 7))
            pe.wait_ge(rw_lo, 1)
            pe.wait_ge(late_set, 1)
            for t in range(NT):
                pe.wait_ge(h2_set, t + 1)
                for half in range(2):
                    if t > 0:
                        pe.wait_ge(h2_lo, 2 * t - 1 + half)
                    for k in range(4):
                        m = pe.transpose(ps[:, half, k * P:(k + 1) * P],
                                         h2[:, t % 2, (4 * half + k) * P:(4 * half + k + 1) * P], ident[:, :])
                    m.then_inc(h2_turned, 1)
                if t > 0:
                    pe.wait_ge(top_set, t)
                for k in range(KT):
                    if k % 4 == 0:
                        pe.wait_ge(h2_lo, 2 * t + 1 + k // 4)
                    m = mm3(ps[:, 2, 0:NE], h2Th[:, k, :], h2Tl[:, k, :], rwh[:, k, :], rwl[:, k, :],
                            k == 0, k == KT - 1)
                m.then_inc(logits_done, 1)
                pe.wait_ge(picked_set, t + 1)
                pe.matmul(ps[:, 3, 0:NE], before[:, :], picked[:, :], start=True, stop=False)
                pe.matmul(ps[:, 3, 0:NE], onesf[:, :], count[:, t, :], start=False, stop=True).then_inc(ranked, 1)
            pe.wait_ge(pos_set, NT)
            pe.matmul(ps[0:NE, 4, 0:1], count[:, NT, :], onesf[:, 0:1], start=True, stop=True).then_inc(jn, 1)
            pe.wait_ge(jn_set, 1)
            pe.matmul(ps[0:NE, 5, 0:1], before[0:NE, 0:NE], nexp[:, 1:2], start=True, stop=True).then_inc(jbase, 1)
            pe.wait_ge(jrows, 1)
            pe.matmul(ps[0:1, 6, 0:3 * JT_W], onesf[0:NE, 0:1],
                      jobr[:, :, :].rearrange("p a b -> p (a b)"), start=True, stop=True).then_inc(jsum, 1)

            def x_turn(r):
                b, half = divmod(r, 2)
                for k in range(4):
                    m = pe.transpose(ps[:, 6 + half, k * P:(k + 1) * P],
                                     xg[:, b, (4 * half + k) * P:(4 * half + k + 1) * P], ident[:, :])
                m.then_inc(x_turned, 1)

            pe.wait_ge(jobs_set, 1)
            pe.wait_ge(gathered, 32)
            for r in range(4):
                if r >= 2:
                    pe.wait_ge(xT_lo, r - 1)
                x_turn(r)

            def job(j, blocks):
                def a_turn(c):
                    for b in range(blocks):
                        pe.wait_ge(act_set[b], j * 4 + c + 1)
                        pe.wait_ge(aT_lo[b], j * 4 + c + 1)
                        for k in range(2):
                            m = pe.transpose(ps[:, 4 + b, k * P:(k + 1) * P], glu[:, b, k * P:(k + 1) * P],
                                             ident[:, :])
                        m.then_inc(a_turned[b], 1)

                def next_x(r):
                    pe.wait_ge(xT_lo, j * 4 + 3 + r)
                    x_turn(r)

                for c in range(JOB_UNITS):
                    sh, sl = (xTh, xTl) if c < 4 else (aTh, aTl)
                    bias = c * UNIT if c < 4 else 2 * FF + (c - 4) * UNIT
                    wh, wl = whis[c % 2], wlos[c % 2]
                    if c == 0:
                        pe.wait_ge(xT_hi, j * 4 + 4)
                        pe.wait_ge(xT_lo, j * 4 + 4)
                        pe.wait_ge(brow1_in, j * 16 + 16)
                    if c == 4:
                        pe.wait_ge(brow2_in, j * 16 + 32)
                    for b in range(blocks):
                        if c < 2:
                            pe.wait_ge(y_set[b], j * 2 + c + 1)
                        else:
                            pe.wait_ge(hid_taken[b], j * 4 + c - 1)
                    for q in range(QUARTERS):
                        pe.wait_ge(split_hi, j * 24 + 4 * (DENSE_UNITS + c) + q + 1)
                        if q < 3:
                            pe.wait_ge(split_lo_dve, j * 18 + 3 * (DENSE_UNITS + c) + q + 1)
                        else:
                            pe.wait_ge(split_lo_pool, j * 6 + DENSE_UNITS + c + 1)
                        for b in range(blocks):
                            if c == 4:
                                pe.wait_ge(aT_lo[b], j * 4 + q + 2)
                            o = ps[:, 2 * b + c % 2, :]
                            if q == 0:
                                pe.matmul(o, ones2[:, :], brow[:, bias:bias + UNIT], start=True, stop=False)
                            for a in range(2):
                                k = 2 * q + a
                                m = mm3(o, sh[:, k, b, :], sl[:, k, b, :], wh[:, q, a, :], wl[:, q, a, :],
                                        False, q == QUARTERS - 1 and a == 1)
                        m.then_inc(quarter_used, 1)
                        if 1 <= c <= 4 and q == 2:
                            a_turn(c - 1)
                        if c == 4 and q == 2:
                            pe.wait_ge(gathered, j * 32 + 64)
                            next_x(0)
                            next_x(1)
                        if c == 5 and q == 0:
                            next_x(2)
                            next_x(3)
                if blocks == 1:
                    pe.sem_inc(a_turned[1], 4)

            for b in range(2):
                pe.sem_inc(a_turned[b], 1)
            with pe.Fori(0, JOBS, 1) as j:
                left = pe.value_load(jobt[0:1, 2, bass.ds(j, 1)], min_val=0, max_val=T)
                with pe.If(left > P):
                    job(j, 2)
                with pe.If(left < P + 1):
                    with pe.If(left > 0):
                        job(j, 1)

        @block.scalar
        def _(act):
            def split(n, q):
                act.wait_ge(raw_in[q], 16 * (n + 1 + 3 * (n >= 2)))
                if n > 0:
                    act.wait_ge(quarter_used, 4 * n + q - 3)
                cols = 256 if n == 3 else UNIT
                act.activation(whi[:, q, :, 0:cols], raw[:, q, :, 0:cols], ACT.Copy).then_inc(split_hi, 1)

            def root(o, i, n):
                act.activation(o, i, ACT.Sqrt, scale=1.0 / n, bias=epsc[:, 0:1]).then_inc(rooted, 1)

            act.wait_ge(eps_set, 1)
            for t in range(NT + 1):
                if t < NT:
                    act.wait_ge(x_in[t], 16)
                    if t > 0:
                        act.wait_ge(squared, t)
                    act.activation(junk0[:, :], xs[:, t, :], ACT.Square, accum_out=ss[:, t:t + 1]).then_inc(squared, 1)
                    act.wait_ge(squared, t + 1)
                    root(rstd[:, t:t + 1], ss[:, t:t + 1], D)
                if t == 1:
                    act.wait_ge(lb_max, 1)
                    act.activation(lbe[:, :, :], lbe[:, :, :], ACT.Exp).then_inc(lb_exp, 1)
                if 2 <= t <= 5:
                    split(0, t - 2)
                if t >= 1:
                    for half in range(2):
                        i = 2 * (t - 1) + half
                        act.wait_ge(turned, i + 1)
                        act.activation(th[:, 4 * half:4 * half + 4, (t - 1) * P:t * P],
                                       ps[:, i % 8, :].rearrange("p (k n) -> p k n", k=4),
                                       ACT.Copy).then_inc(turned_hi, 1)
            act.wait_ge(bias_in, 16 * 5)
            act.activation(bph[:, :], bp[:, :], ACT.Copy).then_inc(bias_hi, 1)

            for n in range(6):
                for q in range(3):
                    split(n + 1, q)
                for c in range(CHAINS[n]):
                    chain_ready(act, n, c)
                    cols = slice((c % 2) * 512, (c % 2) * 512 + 512)
                    if n == 0:
                        act.activation(hf[:, c // 2, cols], ps[:, c, :], ACT.Sigmoid,
                                       bias=bcol[:, 9 + c // 2:10 + c // 2]).then_inc(taken_act, 1)
                    elif n == 1:
                        act.activation(hq[:, c // 2, cols], ps[:, c, :], ACT.Sigmoid,
                                       bias=bcol[:, 5 + c // 2:6 + c // 2]).then_inc(taken_act, 1)
                    elif n == 3 and c >= 2:
                        act.wait_ge(tinit_out, 16)
                        act.activation(av[:, 4 * (c - 2):4 * (c - 2) + 4, :],
                                       ps[:, c, :].rearrange("p (t n) -> p t n", t=4),
                                       ACT.Copy).then_inc(taken_act, 1)
                    elif n == 4:
                        act.activation(hv[:, c, :], ps[:, c, :], ACT.Copy).then_inc(taken_act, 1)
                    elif n == 5:
                        if c >= 2:
                            act.wait_ge(hg_out[c % 2], 16 * (c // 2))
                        act.activation(hgs[:, c % 2, :], ps[:, c, :], ACT.Sigmoid).then_inc(taken_act, 1)
                split(n + 1, 3)

            def exps(b):
                kv = b % 2
                act.wait_ge(maxed, b + 1)
                lo = P if b < 2 else 0
                for i in range(GROUP):
                    m = act.activation(score[:, kv, i, lo:], score[:, kv, i, lo:], ACT.Exp,
                                       bias=stat[:, 1, b, i:i + 1], accum_out=stat[:, 3, b, i:i + 1])
                m.then_inc(exped, 1)
                act.activation(stat[:, 4, b, :], stat[:, 2, b, :], ACT.Exp).then_inc(sinked, 1)

            exps(0)
            for b in range(2 * NT):
                if b + 1 < 2 * NT:
                    exps(b + 1)
                if b < 2:
                    act.sem_inc(pT_act, 1)
                else:
                    act.wait_ge(probs_turned, 2 * b + 1)
                    act.wait_ge(heads_done, b)
                    act.activation(probT[:, 0, :, :], ps[:, 4, :].rearrange("p (i n) -> p i n", i=GROUP),
                                   ACT.Copy).then_inc(pT_act, 1)

            for hd in range(HH):
                act.wait_ge(keys_set, hd + 1)
                act.activation(hf[:, hd, :], hf[:, hd, :], ACT.Ln).then_inc(logs_set, 1)

            def outs(hd):
                act.wait_ge(level_used, STEPS * (hd + 1))
                for i in range(2):
                    act.activation(mix[:, 4 * i:4 * i + 4, ATTN_W + hd * P:ATTN_W + (hd + 1) * P],
                                   ps[:, 2 + i, :].rearrange("p (t n) -> p t n", t=4),
                                   ACT.Copy).then_inc(rec_out, 1)

            for s in range(STEPS * HH):
                hd, L = divmod(s, STEPS)
                if L < LEVELS + 1:
                    act.wait_ge(arg_set, args_by(s))
                    act.activation(he[:, s % 2, :], he[:, s % 2, :], ACT.Exp).then_inc(exp_set, 1)
                else:
                    act.wait_ge(prod_dve, dve_prods_by(s - 2))
                    act.wait_ge(prod_pool, pool_prods_by(s - 2))
                    act.activation(he[:, s % 2, :], hf[:, hd, :], ACT.Exp).then_inc(exp_set, 1)
                    act.wait_ge(level_used, STEPS * hd + LEVELS + 1)
                    if hd > 0:
                        act.wait_ge(added_state, hd)
                    for i in range(2):
                        act.activation(kbT[:, 4 * i:4 * i + 4, :],
                                       ps[:, 4 + i, :].rearrange("p (t n) -> p t n", t=4),
                                       ACT.Copy).then_inc(kbT_set, 1)
                if L == 1 and hd > 0:
                    outs(hd - 1)
            outs(HH - 1)

            k = 0
            act.wait_ge(rec_out, 2 * HH)
            act.wait_ge(level_used, STEPS * HH)
            for t in range(NT):
                for g in range(5):
                    cols = slice(0, ATTN_W) if g == 0 else slice(ATTN_W + (g - 1) * P, ATTN_W + g * P)
                    if k > 0:
                        act.wait_ge(msq, k)
                    act.activation(junk[:, 0:cols.stop - cols.start], mix[:, t, cols], ACT.Square,
                                   accum_out=ssa[:, t, g:g + 1]).then_inc(msq, 1)
                    k += 1
            act.wait_ge(msq, 5 * NT)
            root(rsa[:, :, 0], ssa[:, :, 0], ATTN_W)
            root(rsa[:, :, 1:], ssa[:, :, 1:], P)
            for i in range(2 * NT):
                t, half = divmod(i, 2)
                act.wait_ge(mturned, i + 1)
                act.activation(mh[:, 4 * half:4 * half + 4, t * P:(t + 1) * P],
                               ps[:, i % 8, :].rearrange("p (k n) -> p k n", k=4),
                               ACT.Copy).then_inc(mturned_hi, 1)
            for q in range(3):
                split(7, q)
            split(7, 3)
            act.wait_ge(late_in, 48)
            act.activation(rwh[:, :, :], rw[:, :, :], ACT.Copy).then_inc(rw_hi, 1)

            def gate(t):
                act.wait_ge(top_set, t + 1)
                act.activation(gexp[:, :], top[:, 0:TOPK], ACT.Exp, bias=ntop[:, 0:1],
                               accum_out=gden[:, 0:1]).then_inc(gate_exp, 1)

            for t in range(NT):
                act.wait_ge(x2_set, t + 1)
                if t > 0:
                    act.wait_ge(sq2, t)
                act.activation(junk[:, :], mix[:, t, :], ACT.Square, accum_out=ss[:, t:t + 1]).then_inc(sq2, 1)
                act.wait_ge(sq2, t + 1)
                root(rstd[:, t:t + 1], ss[:, t:t + 1], D)
            for t in range(NT):
                for half in range(2):
                    act.wait_ge(h2_turned, 2 * t + half + 1)
                    if t > 0 and half == 0:
                        act.wait_ge(logits_done, t)
                    act.activation(h2Th[:, 4 * half:4 * half + 4, :],
                                   ps[:, half, :].rearrange("p (k n) -> p k n", k=4),
                                   ACT.Copy).then_inc(h2_hi, 1)
                gate(t)

            def jsplit(j, c, q):
                s = c % 2
                act.wait_ge((raw_in, raw2_in)[s][q], j * 48 + 16 * (c // 2 + 1 + (0 if s else DENSE_UNITS + 3)))
                act.wait_ge(quarter_used, j * 24 + 4 * (DENSE_UNITS + c) + q - 7)
                act.activation(whis[s][:, q, :, :], raws[s][:, q, :, :], ACT.Copy).then_inc(split_hi, 1)

            def xT(j, r):
                b, half = divmod(r, 2)
                act.wait_ge(x_turned, j * 4 + r + 1)
                act.activation(xTh[:, 4 * half:4 * half + 4, b, :],
                               ps[:, 6 + half, :].rearrange("p (k n) -> p k n", k=4),
                               ACT.Copy).then_inc(xT_hi, 1)

            def sigmoid(j, c, b):
                act.wait_ge(glu_set[b], j * 4 + c + 1)
                act.activation(sig[:, b, :], glu[:, b, :], ACT.Sigmoid, scale=ALPHA).then_inc(sig_set[b], 1)

            def aT(j, c, b):
                act.wait_ge(a_turned[b], j * 4 + c + 2)
                act.activation(aTh[:, 2 * c:2 * c + 2, b, :],
                               ps[:, 4 + b, 0:256].rearrange("p (k n) -> p k n", k=2),
                               ACT.Copy).then_inc(aT_hi[b], 1)

            def y_out(j, c, b):
                act.wait_ge(quarter_used, j * 24 + 4 * (DENSE_UNITS + c) + 4)
                if c == 4 and b == 0:
                    act.wait_ge(tcur_set, j + 1)
                act.activation(y[:, b, (c - 4) * UNIT:(c - 3) * UNIT], ps[:, 2 * b + c % 2, :], ACT.Copy,
                               scale=gcur[:, b:b + 1]).then_inc(y_set[b], 1)

            def job(j, blocks):
                for c in range(JOB_UNITS):
                    for b in range(blocks):
                        if 1 <= c <= 4:
                            sigmoid(j, c - 1, b)
                        if c == 5:
                            y_out(j, 4, b)
                    if c == 1:
                        e = act.value_load(jobt[0:1, 0, bass.ds(j, 1)], min_val=0, max_val=NE - 1)
                        act.wait_ge(quarter_used, j * 24 + 4 * DENSE_UNITS)
                        act.wait_ge(brow2_in, j * 16 + 16)
                        act.dma_start(brow[:, 2 * FF:BW].bitcast(F32),
                                      bias_part(e, slice(2 * FF, BW))).then_inc(brow2_in, 16)
                    if c == 5:
                        en = act.value_load(jobt[0:1, 0, bass.ds(j + 1, 1)], min_val=0, max_val=NE - 1)
                        act.wait_ge(quarter_used, j * 24 + 4 * (DENSE_UNITS + 4))
                        act.wait_ge(brow1_in, j * 16 + 16)
                        act.dma_start(brow[:, 0:2 * FF].bitcast(F32),
                                      bias_part(en, slice(0, 2 * FF))).then_inc(brow1_in, 16)
                    jsplit(j, c + 2, 0)
                    if c == 5:
                        xT(j + 1, 2)
                        xT(j + 1, 3)
                    jsplit(j, c + 2, 1)
                    for b in range(blocks):
                        if 1 <= c <= 4:
                            aT(j, c - 1, b)
                    if c == 4:
                        xT(j + 1, 0)
                        xT(j + 1, 1)
                    jsplit(j, c + 2, 2)
                    jsplit(j, c + 2, 3)
                for b in range(blocks):
                    y_out(j, 5, b)
                if blocks == 1:
                    act.sem_inc(sig_set[1], 4)
                    act.sem_inc(aT_hi[1], 4)
                    act.sem_inc(y_set[1], 2)
                with act.If(act.value_load(jobt[0:1, 2, bass.ds(j + 1, 1)], min_val=0, max_val=T) < 1):
                    act.wait_ge(brow1_in, j * 16 + 32)
                    act.sem_inc(act_mark, 1)

            act.wait_ge(jobs_set, 1)
            act.wait_ge(quarter_used, 4 * DENSE_UNITS)
            e0 = act.value_load(jobt[0:1, 0, 0:1], min_val=0, max_val=NE - 1)
            act.dma_start(brow[:, 0:2 * FF].bitcast(F32), bias_part(e0, slice(0, 2 * FF))).then_inc(brow1_in, 16)
            act.wait_ge(acc_out, 16 * NT)
            for i in range(2):
                act.wait_ge(h2_out[i], 16 * NT // 2)
            for q in range(QUARTERS):
                jsplit(0, 0, q)
            for r in range(4):
                xT(0, r)
            for q in range(QUARTERS):
                jsplit(0, 1, q)
            for b in range(2):
                act.sem_inc(y_set[b], 2)
            act.sem_inc(brow2_in, 16)
            with act.Fori(0, JOBS, 1) as j:
                left = act.value_load(jobt[0:1, 2, bass.ds(j, 1)], min_val=0, max_val=T)
                with act.If(left > P):
                    job(j, 2)
                with act.If(left < P + 1):
                    with act.If(left > 0):
                        job(j, 1)
            act.activation(ss[:, 0:1], epsc[:, :], ACT.Copy).then_inc(jobs_over, 1)

            for t in range(NT):
                act.wait_ge(fin_in[t], 16)
                if t > 0:
                    act.wait_ge(fsq, t)
                act.activation(junk[:, :], mix[:, t, :], ACT.Square, accum_out=ss[:, t:t + 1]).then_inc(fsq, 1)
                act.wait_ge(fsq, t + 1)
                root(rstd[:, t:t + 1], ss[:, t:t + 1], D)

        @block.vector
        def _(dve):
            steps = [0]

            def link(ins):
                steps[0] += 1
                ins.then_inc(dve_step, 1)
                dve.wait_ge(dve_step, steps[0])

            def invert(o, roots):
                dve.wait_ge(rooted, roots)
                link(dve.reciprocal(o, o))

            def split(n, q):
                cols = 256 if n == 3 else UNIT
                dve.wait_ge(split_hi, 4 * n + q + 1)
                dve.tensor_tensor(wlo[:, q, :, 0:cols], raw[:, q, :, 0:cols], whi[:, q, :, 0:cols].bitcast(F32),
                                  ALU.subtract).then_inc(split_lo_dve, 1)

            dve.memset(bp[:, :], 0.0).then_inc(bp_zero, 1)

            dve.wait_ge(const_in, 16 * N_CONST)
            for t in range(NT + 1):
                if t < NT:
                    invert(rstd[:, t:t + 1], t + 1)
                    dve.scalar_tensor_tensor(out=xs[:, t, :], in0=xs[:, t, :], scalar=rstd[:, t:t + 1],
                                             in1=grow[:, :], op0=ALU.mult, op1=ALU.mult).then_inc(normed, 1)
                if t == 0:
                    link(dve.tensor_tensor(lbm[:, :], lbl[:, 0, :], lbl[:, 1, :], ALU.max))
                    dve.tensor_tensor(lbe[:, 0, :], lbl[:, 0, :], lbm[:, :], ALU.subtract)
                    dve.tensor_tensor(lbe[:, 1, :], lbl[:, 1, :], lbm[:, :], ALU.subtract).then_inc(lb_max, 1)
                if t == 2:
                    dve.wait_ge(lb_exp, 1)
                    link(dve.tensor_tensor(lbm[:, :], lbe[:, 0, :], lbe[:, 1, :], ALU.add))
                    link(dve.reciprocal(lbm[:, :], lbm[:, :]))
                    link(dve.tensor_tensor(lb[:, :], lbe[:, 0, :], lbm[:, :], ALU.mult))
                    link(dve.tensor_scalar(oml[:, :], lb[:, :], -1.0, 1.0, ALU.mult, ALU.add))
                if 3 <= t <= 5:
                    split(0, t - 3)
                if t >= 1:
                    for half in range(2):
                        i = 2 * (t - 1) + half
                        dve.wait_ge(turned_hi, i + 1)
                        hi = th[:, 4 * half:4 * half + 4, (t - 1) * P:t * P].bitcast(F32)
                        dve.tensor_tensor(tl[:, 4 * half:4 * half + 4, (t - 1) * P:t * P],
                                          ps[:, i % 8, :].rearrange("p (k n) -> p k n", k=4), hi,
                                          ALU.subtract).then_inc(turned_lo, 1)

            for n in range(6):
                for q in range(3):
                    split(n + 1, q)
                for c in range(CHAINS[n]):
                    chain_ready(dve, n, c)
                    cols = slice((c % 2) * 512, (c % 2) * 512 + 512)
                    if n == 1:
                        dve.wait_ge(taken_act, sum(BY_ACT[:n]) + c + 1)
                        dve.scalar_tensor_tensor(out=hq[:, c // 2, cols], in0=ps[:, c, :],
                                                 scalar=bcol[:, 5 + c // 2:6 + c // 2], in1=hq[:, c // 2, cols],
                                                 op0=ALU.add, op1=ALU.mult).then_inc(taken_dve, 1)
                    elif n == 2:
                        dve.wait_ge(bias_out, 32)
                        dve.tensor_scalar(aq[:, c // 2, cols], ps[:, c, :], bcol[:, c // 2:c // 2 + 1],
                                          HD ** -0.5, ALU.add, ALU.mult).then_inc(taken_dve, 1)
                    elif n == 3 and c < 2:
                        dve.wait_ge(tinit_out, 16)
                        dve.tensor_scalar(ak[:, P + c * 512:P + c * 512 + 512], ps[:, c, :], bcol[:, 4:5],
                                          None, ALU.add).then_inc(taken_dve, 1)
                    elif n == 5:
                        dve.wait_ge(taken_act, sum(BY_ACT[:n]) + c + 1)
                        dve.tensor_tensor(hgs[:, c % 2, :], ps[:, c, :], hgs[:, c % 2, :],
                                          ALU.mult).then_inc(taken_dve, 1)

            dve.wait_ge(quarter_used, 4 * 6)
            dve.wait_ge(const_set, 2)
            for h in range(NQ):
                link(dve.scalar_tensor_tensor(out=alibi[:, h, :], in0=dist[:, :], scalar=-SLOPES[h],
                                              in1=closed[:, :], op0=ALU.mult, op1=ALU.add))

            def add_bias(b):
                n, kv = divmod(b, 2)
                dve.wait_ge(scored, b + 1)
                if b >= 2:
                    dve.wait_ge(probs_turned, 2 * b - 2)
                lo = P if n == 0 else 0
                s = score[:, kv, :, lo:]
                link(dve.tensor_tensor(s, ps[:, 2 * kv:2 * kv + 2, :].rearrange("p a (i k) -> p (a i) k", i=2)[:, :, lo:],
                                       alibi[:, GROUP * kv:GROUP * kv + GROUP, lo:], ALU.add))
                dve.sem_inc(score_added, 1)
                link(dve.tensor_reduce(stat[:, 0, b, :], s, AX, ALU.max))
                link(dve.tensor_tensor(stat[:, 0, b, :], stat[:, 0, b, :], sinks[:, GROUP * kv:GROUP * kv + GROUP], ALU.max))
                dve.tensor_scalar(stat[:, 1, b, :], stat[:, 0, b, :], -1.0, None, ALU.mult)
                link(dve.tensor_tensor(stat[:, 2, b, :], sinks[:, GROUP * kv:GROUP * kv + GROUP], stat[:, 0, b, :], ALU.subtract))
                dve.sem_inc(maxed, 1)

            add_bias(0)
            for b in range(2 * NT):
                n, kv = divmod(b, 2)
                if b + 1 < 2 * NT:
                    add_bias(b + 1)
                dve.wait_ge(exped, b + 1)
                dve.wait_ge(sinked, b + 1)
                link(dve.tensor_tensor(stat[:, 3, b, :], stat[:, 3, b, :], stat[:, 4, b, :], ALU.add))
                link(dve.reciprocal(stat[:, 5, b, :], stat[:, 3, b, :]))
                dve.wait_ge(probs_turned, 2 * b + 2)
                if b >= 1:
                    dve.wait_ge(heads_done, b)
                dve.tensor_copy(probT[:, 1, :, :], ps[:, 5, :].rearrange("p (i n) -> p i n", i=GROUP)).then_inc(pT_dve, 1)
                dve.wait_ge(heads_done, b + 1)
                dve.tensor_tensor(mix[:, n, kv * 256:kv * 256 + 256].rearrange("p (i d) -> p i d", i=GROUP),
                                  ps[:, 6 + kv, 0:256].rearrange("p (i d) -> p i d", i=GROUP),
                                  stat[:, 5, b, :].unsqueeze(2).broadcast_to([P, GROUP, HD]),
                                  ALU.mult).then_inc(heads_out, 1)

            for hd in range(HH):
                link(dve.tensor_scalar(hf[:, hd, :], hf[:, hd, :], oml[:, hd:hd + 1], lb[:, hd:hd + 1], ALU.mult, ALU.add))
                dve.tensor_scalar(hk[:, hd, :], hf[:, hd, :], -1.0, 1.0, ALU.mult, ALU.add).then_inc(keys_set, 1)
            dve.wait_ge(reset_set, 1)
            for hd in range(HH):
                dve.wait_ge(logs_set, hd + 1)
                dve.tensor_tensor_scan(hf[:, hd, :], reset[:, :], hf[:, hd, :], 0.0, ALU.mult, ALU.add).then_inc(sums_set, 1)
            dve.wait_ge(sums_set, HH)

            def args(s):
                hd, L = divmod(s, STEPS)
                e = he[:, s % 2, :]
                b = hf[:, hd, :]
                if s >= 2:
                    dve.wait_ge(prod_pool, pool_prods_by(s - 2))
                    dve.wait_ge(prod_dve, dve_prods_by(s - 2))
                if L < LEVELS:
                    h = 64 >> L
                    bv, ev = (z.rearrange("p (m two h) -> p m two h", two=2, h=h) for z in (b, e))
                    mid = bv[:, :, 0, h - 1:h].broadcast_to([P, T // (2 * h), h])
                    dve.tensor_tensor(ev[:, :, 1, :], bv[:, :, 1, :], mid, ALU.subtract)
                    dve.tensor_tensor(ev[:, :, 0, :], mid, bv[:, :, 0, :], ALU.subtract).then_inc(arg_set, 1)
                elif L == LEVELS:
                    bv, ev = (z.rearrange("p (t n) -> p t n", n=P) for z in (b, e))
                    dve.tensor_tensor(ev, bv[:, :, P - 1:P].broadcast_to([P, NT, P]), bv, ALU.subtract).then_inc(arg_set, 1)

            def prods(s):
                hd, L = divmod(s, STEPS)
                dve.wait_ge(exp_set, s + 1)
                if s >= 2:
                    dve.wait_ge(level_used, s - 1)
                if L < LEVELS:
                    h = 64 >> L
                    ov, qv, ev = (z.rearrange("p (m two h) -> p m two h", two=2, h=h)[:, :, 1, :]
                                  for z in (hp[:, s % 2, :], hq[:, hd, :], he[:, s % 2, :]))
                    dve.tensor_tensor(ov, qv, ev, ALU.mult).then_inc(prod_dve, 1)
                elif L == LEVELS + 1:
                    dve.tensor_copy(decay[:, :], he[:, s % 2, :].rearrange("p (t n) -> p t n", n=P)[:, :, P - 1])
                    link(dve.tensor_tensor(hp[:, s % 2, :], hq[:, hd, :], he[:, s % 2, :], ALU.mult))
                    dve.sem_inc(prod_dve, 1)

            def copies(s):
                hd, L = divmod(s, STEPS)
                a = attT[hd % 2]
                if L < LEVELS:
                    lev = LEVELS * hd + L
                    h = 64 >> L
                    if L == 0:
                        dve.wait_ge(diag_done, hd + 1)
                        link(dve.tensor_tensor(a[:, :, :], ps[:, 2:4, :].rearrange("p a (t n) -> p (a t) n", n=P),
                                               ident[:, :].unsqueeze(1).broadcast_to([P, NT, P]), ALU.mult))
                    dve.wait_ge(level_used, s + 1)
                    nb = 64 // h
                    link(dve.copy_predicated(
                        a[:, :, :].rearrange("p t (m two h) -> p t m two h", two=2, h=h)[:, :, :, 1, :],
                        maskL[:, L, :].rearrange("p (m h) -> p m h", h=h).unsqueeze(1).broadcast_to([P, NT, nb, h]),
                        ps[:, lev % 2, :].rearrange("p (t m h) -> p t m h", t=NT, h=h)))
                    dve.sem_inc(level_copied, 1)
                elif L == LEVELS + 1:
                    dve.wait_ge(added_state, hd + 1)
                    if hd > 0:
                        dve.wait_ge(level_used, STEPS * hd)
                    link(dve.tensor_copy(state[:, 0, :], ps[:, 6, 0:P]))
                    for t in range(1, NT - 1):
                        link(dve.scalar_tensor_tensor(out=state[:, t, :], in0=state[:, t - 1, :], scalar=decay[:, t:t + 1],
                                                      in1=ps[:, 6 + t // 4, (t % 4) * P:(t % 4 + 1) * P],
                                                      op0=ALU.mult, op1=ALU.add))
                    dve.sem_inc(states_set, 1)

            for s in range(STEPS * HH + 2):
                if s < STEPS * HH:
                    args(s)
                if 1 <= s <= STEPS * HH:
                    prods(s - 1)
                if s >= 2:
                    copies(s - 2)

            invert(rsa[:, :, :], NT + 2)
            dve.wait_ge(gmix_in, 32)
            dve.wait_ge(hgt_set, 1)
            for t in range(NT + 1):
                if t < NT:
                    o = mix[:, t, ATTN_W:]
                    link(dve.tensor_tensor(o.rearrange("p (h n) -> p h n", h=HH), o.rearrange("p (h n) -> p h n", h=HH),
                                           rsa[:, t, 1:].unsqueeze(2).broadcast_to([P, HH, P]), ALU.mult))
                    dve.tensor_tensor(o, o, hgt[:, t, :], ALU.mult)
                    link(dve.scalar_tensor_tensor(out=mix[:, t, 0:ATTN_W], in0=mix[:, t, 0:ATTN_W], scalar=rsa[:, t, 0:1],
                                                  in1=grow[:, 0:ATTN_W], op0=ALU.mult, op1=ALU.mult))
                    dve.sem_inc(mnormed, 1)
                if t >= 1:
                    for half in range(2):
                        i = 2 * (t - 1) + half
                        dve.wait_ge(mturned_hi, i + 1)
                        dve.tensor_tensor(ml[:, 4 * half:4 * half + 4, (t - 1) * P:t * P],
                                          ps[:, i % 8, :].rearrange("p (k n) -> p k n", k=4),
                                          mh[:, 4 * half:4 * half + 4, (t - 1) * P:t * P].bitcast(F32),
                                          ALU.subtract).then_inc(mturned_lo, 1)
            for q in range(3):
                split(7, q)
            dve.wait_ge(xr_in, 16)
            for c in range(8):
                chain_ready(dve, 6, c)
                dve.tensor_tensor(mix[:, c, 0:UNIT], mix[:, c, 0:UNIT], ps[:, c, :], ALU.add).then_inc(taken_dve, 1)
            dve.wait_ge(rw_hi, 1)
            dve.tensor_tensor(rwl[:, :, :], rw[:, :, :], rwh[:, :, :].bitcast(F32), ALU.subtract).then_inc(rw_lo, 1)
            dve.wait_ge(late_set, 1)
            link(dve.memset(count[:, 0, :], 0.0))
            for c in range(8):
                chain_ready(dve, 7, c)
                link(dve.tensor_tensor(mix[:, c, UNIT:], mix[:, c, UNIT:], ps[:, c, :], ALU.add))
                dve.sem_inc(taken_dve, 1)
                dve.sem_inc(x2_set, 1)

            for t in range(NT):
                invert(rstd[:, t:t + 1], NT + 2 + t + 1)
                if t >= 2:
                    dve.wait_ge(h2_out[t % 2], 16 * (t // 2))
                dve.scalar_tensor_tensor(out=h2[:, t % 2, :], in0=mix[:, t, :], scalar=rstd[:, t:t + 1],
                                         in1=g2row[:, :], op0=ALU.mult, op1=ALU.mult).then_inc(h2_set, 1)
                for half in range(2):
                    dve.wait_ge(h2_hi, 2 * t + half + 1)
                    dve.tensor_tensor(h2Tl[:, 4 * half:4 * half + 4, :],
                                      ps[:, half, :].rearrange("p (k n) -> p k n", k=4),
                                      h2Th[:, 4 * half:4 * half + 4, :].bitcast(F32), ALU.subtract).then_inc(h2_lo, 1)
                dve.wait_ge(logits_done, t + 1)
                if t > 0:
                    dve.wait_ge(gate_exp, t)
                link(dve.tensor_tensor(logit[:, :], ps[:, 2, 0:NE], rb[:, :], ALU.add))
                link(dve.max(top[:, :], logit[:, :]))
                dve.max_index(topi[:, :], top[:, :], logit[:, :])
                link(dve.tensor_scalar(ntop[:, :], top[:, 0:1], -1.0, None, ALU.mult))
                dve.sem_inc(top_set, 1)
                link(dve.tensor_copy(topf[:, :], topi[:, :]))
                link(dve.tensor_tensor(hot[:, :, :], iotaE[:, :].unsqueeze(1).broadcast_to([P, TOPK, NE]),
                                       topf[:, 0:TOPK].unsqueeze(2).broadcast_to([P, TOPK, NE]), ALU.is_equal))
                link(dve.tensor_reduce(picked[:, :], hot[:, :, :].rearrange("p k e -> p e k"), AX, ALU.add))
                dve.sem_inc(picked_set, 1)
                link(dve.tensor_tensor(count[:, t + 1, :], count[:, t, :], picked[:, :], ALU.add))
                dve.wait_ge(ranked, t + 1)
                link(dve.tensor_tensor(hot[:, :, :], hot[:, :, :],
                                       ps[:, 3, 0:NE].unsqueeze(1).broadcast_to([P, TOPK, NE]), ALU.mult))
                link(dve.tensor_reduce(rank[:, :], hot[:, :, :], AX, ALU.add))
                link(dve.scalar_tensor_tensor(out=pos[:, t, :], in0=topf[:, 0:TOPK], scalar=float(T), in1=rank[:, :],
                                              op0=ALU.mult, op1=ALU.add))
                dve.wait_ge(gate_exp, t + 1)
                link(dve.reciprocal(grec[:, :], gden[:, :]))
                dve.tensor_scalar(load[:, t, :, 1], gexp[:, :], grec[:, 0:1], None, ALU.mult)
                link(dve.tensor_copy(load[:, t, :, 0], tok[:, t:t + 1].broadcast_to([P, TOPK])))
                dve.sem_inc(pos_set, 1)

            dve.wait_ge(jn, 1)
            link(dve.tensor_copy(nexp[:, 0:1], ps[0:NE, 4, 0:1]))
            link(dve.tensor_scalar(nexp[:, 1:2], nexp[:, 0:1], 0.0, None, ALU.is_gt))
            for k in range(1, T // JOB_T):
                link(dve.scalar_tensor_tensor(out=nexp[:, 1:2], in0=nexp[:, 0:1], scalar=float(k * JOB_T), in1=nexp[:, 1:2],
                                              op0=ALU.is_gt, op1=ALU.add))
            dve.sem_inc(jn_set, 1)
            dve.wait_ge(jbase, 1)
            link(dve.tensor_copy(nexp[:, 2:3], ps[0:NE, 5, 0:1]))
            link(dve.tensor_scalar(jobm[:, 0, :], jobi[:, :], nexp[:, 2:3], None, ALU.subtract))
            link(dve.tensor_scalar(jobm[:, 1, :], jobm[:, 0, :], 0.0, None, ALU.is_ge))
            link(dve.scalar_tensor_tensor(out=jobm[:, 1, :], in0=jobm[:, 0, :], scalar=nexp[:, 1:2], in1=jobm[:, 1, :],
                                          op0=ALU.is_lt, op1=ALU.mult))
            dve.tensor_scalar(jobr[:, 0, :], jobm[:, 1, :], eid[:, 0:1], None, ALU.mult)
            link(dve.tensor_scalar(nexp[:, 3:4], eid[:, 0:1], float(T // JOB_T), None, ALU.mult))
            dve.scalar_tensor_tensor(out=jobr[:, 1, :], in0=jobm[:, 0, :], scalar=nexp[:, 3:4], in1=jobm[:, 1, :],
                                     op0=ALU.add, op1=ALU.mult)
            link(dve.tensor_scalar(jobr[:, 2, :], jobm[:, 0, :], -float(JOB_T), nexp[:, 0:1], ALU.mult, ALU.add))
            link(dve.tensor_tensor(jobr[:, 2, :], jobr[:, 2, :], jobm[:, 1, :], ALU.mult))
            dve.sem_inc(jrows, 1)
            dve.wait_ge(jsum, 1)
            dve.tensor_copy(jobt[:, :, :].rearrange("p a b -> p (a b)"), ps[0:1, 6, 0:3 * JT_W]).then_inc(jobs_set, 1)
            dve.wait_ge(jobs_set, 1)

            def jsplit(j, c, q):
                s = c % 2
                dve.wait_ge(split_hi, j * 24 + 4 * (DENSE_UNITS + c) + q + 1)
                dve.tensor_tensor(wlos[s][:, q, :, :], raws[s][:, q, :, :], whis[s][:, q, :, :].bitcast(F32),
                                  ALU.subtract).then_inc(split_lo_dve, 1)

            def xT(j, r):
                b, half = divmod(r, 2)
                dve.wait_ge(xT_hi, j * 4 + r + 1)
                k = slice(4 * half, 4 * half + 4)
                dve.tensor_tensor(xTl[:, k, b, :], ps[:, 6 + half, :].rearrange("p (k n) -> p k n", k=4),
                                  xTh[:, k, b, :].bitcast(F32), ALU.subtract).then_inc(xT_lo, 1)

            def hidden(j, c, blocks):
                dve.wait_ge(quarter_used, j * 24 + 4 * (DENSE_UNITS + c) + 4)
                for b in range(blocks):
                    hid = ps[:, 2 * b + c % 2, :].rearrange("p (n two) -> p n two", two=2)
                    dve.wait_ge(a_turned[b], j * 4 + c + 1)
                    dve.tensor_scalar(glu[:, b, :], hid[:, :, 0], LIMIT, None, ALU.min).then_inc(glu_set[b], 1)
                    dve.tensor_scalar(lin[:, b, :], hid[:, :, 1], LIMIT, 1.0, ALU.min, ALU.add).then_inc(hid_taken[b], 1)
                for b in range(blocks):
                    dve.wait_ge(hid_taken[b], j * 4 + c + 1)
                    dve.scalar_tensor_tensor(out=lin[:, b, :], in0=lin[:, b, :], scalar=1.0 - LIMIT, in1=glu[:, b, :],
                                             op0=ALU.max, op1=ALU.mult).then_inc(prod_set[b], 1)

            def aT(j, c, b):
                dve.wait_ge(aT_hi[b], j * 4 + c + 1)
                dve.tensor_tensor(aTl[:, 2 * c:2 * c + 2, b, :], ps[:, 4 + b, 0:256].rearrange("p (k n) -> p k n", k=2),
                                  aTh[:, 2 * c:2 * c + 2, b, :].bitcast(F32), ALU.subtract).then_inc(aT_lo[b], 1)

            def job(j, blocks):
                for c in range(JOB_UNITS):
                    if 1 <= c <= 4:
                        hidden(j, c - 1, blocks)
                    jsplit(j, c + 2, 0)
                    if c == 5:
                        xT(j + 1, 2)
                        xT(j + 1, 3)
                    jsplit(j, c + 2, 1)
                    for b in range(blocks):
                        if 1 <= c <= 4:
                            aT(j, c - 1, b)
                    if c == 4:
                        xT(j + 1, 0)
                        xT(j + 1, 1)
                    jsplit(j, c + 2, 2)
                if blocks == 1:
                    for done in (glu_set, hid_taken, prod_set, aT_lo):
                        dve.sem_inc(done[1], 4)

            for q in range(3):
                jsplit(0, 0, q)
            dve.memset(y[:, 1, :], 0.0).then_inc(y_zero, 1)
            for r in range(4):
                xT(0, r)
            for q in range(3):
                jsplit(0, 1, q)
            for b in range(2):
                dve.sem_inc(aT_lo[b], 1)
            with dve.Fori(0, JOBS, 1) as j:
                left = dve.value_load(jobt[0:1, 2, bass.ds(j, 1)], min_val=0, max_val=T)
                with dve.If(left > P):
                    job(j, 2)
                with dve.If(left < P + 1):
                    with dve.If(left > 0):
                        job(j, 1)
            dve.memset(ss[:, 1:2], 0.0).then_inc(jobs_over, 1)

            dve.wait_ge(gfin_in, 16)
            for t in range(NT):
                invert(rstd[:, t:t + 1], 2 * NT + 2 + t + 1)
                dve.scalar_tensor_tensor(out=mix[:, t, :], in0=mix[:, t, :], scalar=rstd[:, t:t + 1],
                                         in1=g2row[:, :], op0=ALU.mult, op1=ALU.mult).then_inc(fset, 1)

        @block.gpsimd
        def _(pool):
            steps = [0]

            def link(ins):
                steps[0] += 1
                ins.then_inc(pool_step, 1)
                pool.wait_ge(pool_step, steps[0])

            def select(o, pattern, cm, base_, fill=0.0, op=ALU.is_ge):
                link(pool.affine_select(out=o, in_=o, compare_op=op, fill=fill, base=base_,
                                        pattern=pattern, channel_multiplier=cm))

            def iota(o, pattern, cm, base_=0):
                link(pool.iota(o, pattern=pattern, base=base_, channel_multiplier=cm,
                               allow_small_or_imprecise_dtypes=True))

            def split(n, q):
                cols = 256 if n == 3 else UNIT
                pool.wait_ge(split_hi, 4 * n + q + 1)
                pool.tensor_tensor(wlo[:, q, :, 0:cols], raw[:, q, :, 0:cols], whi[:, q, :, 0:cols].bitcast(F32),
                                   ALU.subtract).then_inc(split_lo_pool, 1)

            pool.memset(epsc[:, :], EPS).then_inc(eps_set, 1)
            link(pool.memset(ident[:, :], 0.0))
            select(ident[:, :], [[-1, P]], 1, 0, 1.0, ALU.not_equal)
            link(pool.memset(ones2[:, :].bitcast(F32), 1.0))
            pool.sem_inc(const_set, 1)
            link(pool.memset(tinit[:, :, :], 0.0))
            iota(tinit[:, :, 0], [[1, JOB_T]], 0, T)
            pool.dma_start(table_d.rearrange("(p n) w -> p n w", p=P), tinit[:, :, :]).then_inc(tinit_out, 16)
            split(0, 3)
            iota(dist[:, :], [[-1, 2 * P]], 1, P)
            link(pool.memset(closed[:, :], 0.0))
            select(closed[:, :], [[-1, 2 * P]], 1, P, NEG)
            select(closed[:, :], [[1, 2 * P]], -1, -1, NEG)
            link(pool.memset(maskL[:, :, :], 1))
            for L in range(LEVELS):
                h = 64 >> L
                m = maskL[:, L, :].rearrange("p (m h) -> p m h", h=h)
                select(m, [[-2 * h, 64 // h], [0, h]], 1, 0)
                select(m, [[2 * h, 64 // h], [0, h]], -1, h - 1)
            link(pool.memset(onesf[:, :], 1.0))
            link(pool.memset(before[:, :], 1.0))
            select(before[:, :], [[1, P]], -1, -1)
            pool.sem_inc(const_set, 1)
            pool.wait_ge(bias_hi, 1)
            pool.tensor_tensor(bpl[:, :], bp[:, :], bph[:, :].bitcast(F32), ALU.subtract).then_inc(bias_lo, 1)
            for n in range(6):
                if n == 5:
                    for c in range(8):
                        pool.wait_ge(*taken(5, c))
                        pool.dma_start(hg_d[c * P:(c + 1) * P, :], hgs[:, c % 2, :]).then_inc(hg_out[c % 2], 16)
                split(n + 1, 3)

            pool.wait_ge(quarter_used, 4 * 6)
            link(pool.memset(reset[:, :], 1.0))
            link(pool.memset(reset[:, :].rearrange("p (t n) -> p t n", n=P)[:, :, 0:1], 0.0))
            pool.sem_inc(reset_set, 1)
            pool.wait_ge(keys_set, HH)
            for s in range(STEPS * HH):
                hd, L = divmod(s, STEPS)
                pool.wait_ge(exp_set, s + 1)
                if s >= 2:
                    pool.wait_ge(level_used, s - 1)
                if L < LEVELS:
                    h = 64 >> L
                    o, k, e = (z.rearrange("p (m two h) -> p m two h", two=2, h=h)[:, :, 0, :]
                               for z in (hp[:, s % 2, :], hk[:, hd, :], he[:, s % 2, :]))
                    pool.tensor_tensor(o, k, e, ALU.mult).then_inc(prod_pool, 1)
                elif L == LEVELS:
                    pool.tensor_tensor(hp[:, s % 2, :], hk[:, hd, :], he[:, s % 2, :], ALU.mult).then_inc(prod_pool, 1)

            pool.wait_ge(hgt_in, 16)
            pool.wait_ge(gmix_in, 32)
            pool.tensor_tensor(hgt[:, :, :], hgt[:, :, :],
                               grow[:, 512:].unsqueeze(1).broadcast_to([P, NT, 512]), ALU.mult).then_inc(hgt_set, 1)
            pool.wait_ge(msq, 5 * NT)
            link(pool.memset(zero[:, :], 0.0))
            pool.sem_inc(zero_set, 1)
            iota(iotaE[:, :], [[1, NE]], 0)
            iota(tok[:, :], [[P, NT]], 1)
            iota(jobi[:, :], [[1, JT_W]], 0)
            iota(eid[:, :], [[0, 1]], 1)
            pool.wait_ge(late_in, 48)
            pool.sem_inc(late_set, 1)
            split(7, 3)
            for t in range(NT):
                pool.wait_ge(pos_set, t + 1)
                for k in range(TOPK):
                    pool.indirect_dma_start(out=table_d, out_offset=bass.IndirectOffsetOnAxis(ap=pos[:, t, k:k + 1], axis=0),
                                            in_=load[:, t, k, :], in_offset=None).then_inc(table_out, 16)
            pool.wait_ge(jobs_set, 1)
            pool.wait_ge(table_out, 16 * NT * TOPK)
            tview = table_d.rearrange("(m p) w -> p m w", p=P)

            def wait(semaphore, value):
                pool.wait_ge(semaphore, value)
                pool.sem_inc(pool_mark, 1)

            def load_slots(j):
                part = pool.value_load(jobt[0:1, 1, bass.ds(j, 1)], min_val=0, max_val=NE * 4 - 1)
                pool.dma_start(tnext[:, :, :], tview[:, bass.ds(part * 2, 2), :]).then_inc(tnext_in, 16)

            def gather(j):
                wait(tnext_in, j * 16 + 16)
                pool.tensor_copy(inext[:, :], tnext[:, :, 0]).then_inc(tnext_cast, 1)
                wait(tnext_cast, j + 1)
                for b in range(2):
                    pool.indirect_dma_start(out=xg[:, b, :], out_offset=None, in_=h2_d,
                                            in_offset=bass.IndirectOffsetOnAxis(ap=inext[:, b:b + 1], axis=0)
                                            ).then_inc(gathered, 16)

            def jsplit(j, c):
                s = c % 2
                wait(split_hi, j * 24 + 4 * (DENSE_UNITS + c) + 4)
                pool.tensor_tensor(wlos[s][:, 3, :, :], raws[s][:, 3, :, :], whis[s][:, 3, :, :].bitcast(F32),
                                   ALU.subtract).then_inc(split_lo_pool, 1)

            def activate(j, c, b):
                wait(prod_set[b], j * 4 + c + 1)
                wait(sig_set[b], j * 4 + c + 1)
                pool.tensor_tensor(glu[:, b, :], lin[:, b, :], sig[:, b, :], ALU.mult).then_inc(act_set[b], 1)

            def job(j, blocks):
                for c in range(JOB_UNITS):
                    for b in range(blocks):
                        if 1 <= c <= 4:
                            activate(j, c - 1, b)
                    if c == 1:
                        with pool.If(j > 0):
                            wait(scattered, j * 32)
                        pool.tensor_copy(icur[:, :], tnext[:, :, 0])
                        pool.tensor_copy(gcur[:, :], tnext[:, :, 1]).then_inc(tcur_set, 1)
                        wait(tcur_set, j + 1)
                        load_slots(j + 1)
                    if c == 2:
                        wait(x_turned, j * 4 + 4)
                        gather(j + 1)
                    jsplit(j, c + 2)
                for b in range(2):
                    if b < blocks:
                        wait(y_set[b], j * 2 + 4)
                    pool.indirect_dma_start(out=acc_d, out_offset=bass.IndirectOffsetOnAxis(ap=icur[:, b:b + 1], axis=0),
                                            in_=y[:, b, :], in_offset=None, compute_op=ALU.add).then_inc(scattered, 16)
                if blocks == 1:
                    pool.sem_inc(act_set[1], 4)
                with pool.If(pool.value_load(jobt[0:1, 2, bass.ds(j + 1, 1)], min_val=0, max_val=T) < 1):
                    wait(scattered, j * 32 + 32)

            pool.wait_ge(h2_out[0], 64)
            pool.wait_ge(h2_out[1], 64)
            pool.wait_ge(acc_out, 128)
            pool.wait_ge(pads_out, 64)
            load_slots(0)
            gather(0)
            jsplit(0, 0)
            jsplit(0, 1)
            pool.wait_ge(y_zero, 1)
            with pool.Fori(0, JOBS, 1) as j:
                left = pool.value_load(jobt[0:1, 2, bass.ds(j, 1)], min_val=0, max_val=T)
                with pool.If(left > P):
                    job(j, 2)
                with pool.If(left < P + 1):
                    with pool.If(left > 0):
                        job(j, 1)
            pool.memset(ss[:, 2:3], 0.0).then_inc(jobs_over, 1)


_INS = ["x", "norm1_g", "w_in", "b_in", "attn_sinks", "attn_out_g", "hgrn_lb_logits", "hgrn_out_g",
        "w_out", "b_out", "norm2_g", "router_w", "router_b", "w1", "b1", "w2", "b2", "final_g"]


def kernel(**inputs):
    import numpy as np
    import concourse.bacc as bacc
    from concourse import mybir
    from concourse.bass_utils import run_bass_kernel_spmd

    nc = bacc.Bacc("TRN2", target_bir_lowering=False, num_devices=1)
    arrays, args = {}, []
    for name in _INS:
        a = np.ascontiguousarray(inputs[name])
        arrays[f"in_{name}"] = a
        args.append(nc.dram_tensor(f"in_{name}", a.shape, mybir.dt.from_np(a.dtype), kind="ExternalInput").ap())
    args.append(nc.dram_tensor("out_0", (1, T, D), mybir.dt.from_np(np.dtype("float32")), kind="ExternalOutput").ap())
    build(nc, *args)
    r = run_bass_kernel_spmd(nc, [arrays], core_ids=[0])
    return r.results[0]["out_0"]
```
